# Optimizing a Trainium2 kernel written in Bass

```python
import math
import jax, jax.numpy as jnp
from jax import lax
import numpy as np

D_MODEL = 1024
BATCH = 1
SEQ = 1024
DEPTH = 1
DEC_BATCH = 8
DEC_SEQ = 8
PAST_LEN = 8192
PAGE_SIZE = 128

D_LRU = D_MODEL // 2
LRU_HEADS = 8
LRU_HD = D_LRU // LRU_HEADS
LRU_CONV = 4
LRU_C = 8.0
D_SC = D_MODEL // 4
SC_CONV = 3
MEM_HEADS = 4
MEM_HD = (D_MODEL // 4) // MEM_HEADS
D_MEM = MEM_HEADS * MEM_HD
N_MEM = 256
D_MIX = D_LRU + D_SC + D_MEM
D_IN = 2 * D_LRU + 3 * D_SC + D_MEM
PEER_HEADS = 8
N_KEYS = 128
N_EXPERTS = N_KEYS * N_KEYS
PEER_DK = 256
PEER_TOPK = 16
PEER_BLOCK = 128
LN_EPS = 1e-5
RMS_EPS = 1e-6
DEEPNORM_ALPHA = (2.0 * DEPTH) ** 0.25
DEEPNORM_BETA = (8.0 * DEPTH) ** -0.25

kernel_name = 'hymba_rglru_shortconv_peer_step'

def _layernorm(x, g, b):
    xf = x.astype(jnp.float32)
    mu = jnp.mean(xf, axis=-1, keepdims=True)
    var = jnp.mean(jnp.square(xf - mu), axis=-1, keepdims=True)
    y = (xf - mu) * lax.rsqrt(var + LN_EPS) * g.astype(jnp.float32) + b.astype(jnp.float32)
    return y.astype(x.dtype)

def _rmsnorm(x, g):
    xf = x.astype(jnp.float32)
    y = xf * lax.rsqrt(jnp.mean(jnp.square(xf), axis=-1, keepdims=True) + RMS_EPS) * g.astype(jnp.float32)
    return y.astype(x.dtype)

def _causal_dwconv(x, buf, w):
    width = w.shape[0]
    s = x.shape[1]
    full = jnp.concatenate([buf.astype(x.dtype), x], axis=1)
    y = full[:, 0:s] * w[0]
    for k in range(1, width):
        y = y + full[:, k:k + s] * w[k]
    return y, full[:, full.shape[1] - (width - 1):]

def _linear_scan(a, b, h0):
    b = b.at[:, 0].add(a[:, 0] * h0)

    def comb(l, r):
        return (l[0] * r[0], r[0] * l[1] + r[1])

    _, h = lax.associative_scan(comb, (a, b), axis=1)
    return h

def _mem_kv(mem, w_mem_kv):
    bsz = mem.shape[0]
    kv = jnp.einsum('bmd,de->bme', mem, w_mem_kv)
    k, v = jnp.split(kv, 2, axis=-1)
    return (k.reshape(bsz, N_MEM, MEM_HEADS, MEM_HD), v.reshape(bsz, N_MEM, MEM_HEADS, MEM_HD))

def _mixer(x, mem_k, mem_v, lru_buf, h0, sc_buf, lp):
    bsz, s, _ = x.shape
    proj = jnp.einsum('bsd,de->bse', x, lp['w_in'])
    cuts = [D_LRU, 2 * D_LRU, 2 * D_LRU + D_SC, 2 * D_LRU + 2 * D_SC, 2 * D_LRU + 3 * D_SC]
    xl, gate, sc_b, sc_c, sc_x, q = jnp.split(proj, cuts, axis=-1)
    xc, new_lru_buf = _causal_dwconv(xl, lru_buf, lp['lru_conv_w'])
    xc = xc + lp['lru_conv_b']
    xh = xc.reshape(bsz, s, LRU_HEADS, LRU_HD)
    r = jax.nn.sigmoid(jnp.einsum('bshi,hij->bshj', xh, lp['w_rg_a']).reshape(bsz, s, D_LRU) + lp['b_rg_a'])
    i = jax.nn.sigmoid(jnp.einsum('bshi,hij->bshj', xh, lp['w_rg_x']).reshape(bsz, s, D_LRU) + lp['b_rg_x'])
    log_a = LRU_C * r.astype(jnp.float32) * jax.nn.log_sigmoid(lp['lru_lambda'].astype(jnp.float32))
    a = jnp.exp(log_a)
    bt = jnp.sqrt(-jnp.expm1(2.0 * log_a)) * (i * xc).astype(jnp.float32)
    h = _linear_scan(a, bt, h0.astype(jnp.float32))
    y_lru = h.astype(x.dtype) * jax.nn.gelu(gate, approximate=False)
    u, new_sc_buf = _causal_dwconv(sc_c * sc_x, sc_buf, lp['sc_conv_w'])
    y_sc = sc_b * u
    qh = q.reshape(bsz, s, MEM_HEADS, MEM_HD)
    sc = jnp.einsum('bshd,bmhd->bhsm', qh, mem_k).astype(jnp.float32) * (MEM_HD ** -0.5)
    p = jax.nn.softmax(sc, axis=-1).astype(x.dtype)
    y_mem = jnp.einsum('bhsm,bmhd->bshd', p, mem_v).reshape(bsz, s, D_MEM)
    y = jnp.concatenate([_rmsnorm(y_lru, lp['g_lru']), _rmsnorm(y_sc, lp['g_sc']), _rmsnorm(y_mem, lp['g_mem'])], axis=-1)
    out = jnp.einsum('bse,ed->bsd', y, lp['w_out'])
    return out, new_lru_buf, h[:, -1], new_sc_buf

def _peer(x, wq, keys, u_tab, v_tab):
    bsz, s, d = x.shape
    t = bsz * s
    n_blk = -(-t // PEER_BLOCK)
    xt = jnp.pad(x.reshape(t, d), ((0, n_blk * PEER_BLOCK - t), (0, 0))).reshape(n_blk, PEER_BLOCK, d)

    def block(xb):
        qb = jnp.einsum('td,de->te', xb, wq).reshape(PEER_BLOCK, PEER_HEADS, 2, PEER_DK // 2)
        sk = jnp.einsum('thpd,hpkd->thpk', qb, keys).astype(jnp.float32)
        v1, i1 = lax.top_k(sk[:, :, 0], PEER_TOPK)
        v2, i2 = lax.top_k(sk[:, :, 1], PEER_TOPK)
        cand = (v1[..., :, None] + v2[..., None, :]).reshape(PEER_BLOCK, PEER_HEADS, PEER_TOPK * PEER_TOPK)
        top_s, ci = lax.top_k(cand, PEER_TOPK)
        e = (jnp.take_along_axis(i1, ci // PEER_TOPK, axis=-1) * N_KEYS
             + jnp.take_along_axis(i2, ci % PEER_TOPK, axis=-1))
        g = jax.nn.softmax(top_s, axis=-1).astype(xb.dtype)
        act = jax.nn.gelu(jnp.einsum('td,thkd->thk', xb, u_tab[e]), approximate=False)
        return jnp.einsum('thk,thkd->td', g * act, v_tab[e])

    out = lax.map(block, xt).reshape(n_blk * PEER_BLOCK, d)[:t]
    return out.reshape(bsz, s, d)

def _layer(x, mem_k, mem_v, lru_buf, h0, sc_buf, lp):
    m, nb, nh, ns = _mixer(x, mem_k, mem_v, lru_buf, h0, sc_buf, lp)
    x = _layernorm(DEEPNORM_ALPHA * x + m, lp['ln1_g'], lp['ln1_b'])
    f = _peer(x, lp['peer_wq'], lp['peer_keys'], lp['peer_u'], lp['peer_v'])
    x = _layernorm(DEEPNORM_ALPHA * x + f, lp['ln2_g'], lp['ln2_b'])
    return x, nb, nh, ns

def setup_inputs(seed: int = 0) -> dict:
    key = jax.random.key(seed)
    ks = jax.random.split(key, 40)
    f32 = jnp.float32
    nrm = lambda k, shape, sc: jax.random.normal(k, shape, f32) * sc
    L = DEPTH
    u_lam = jax.random.uniform(ks[10], (L, D_LRU), f32, 0.9, 0.999)
    s_lam = u_lam ** (1.0 / LRU_C)
    lam = jnp.log(s_lam) - jnp.log1p(-s_lam)
    w_k = nrm(ks[13], (L, D_MODEL, D_MEM), D_MODEL ** -0.5)
    w_v = nrm(ks[14], (L, D_MODEL, D_MEM), DEEPNORM_BETA * D_MODEL ** -0.5)
    return {
        'x_prompt': nrm(ks[0], (BATCH, SEQ, D_MODEL), 1.0),
        'x_sample': nrm(ks[1], (DEC_BATCH, DEC_SEQ, D_MODEL), 1.0),
        'mem_prompt': nrm(ks[2], (BATCH, N_MEM, D_MODEL), 1.0),
        'cache_mem_k': nrm(ks[3], (L, DEC_BATCH, N_MEM, MEM_HEADS, MEM_HD), 1.0),
        'cache_mem_v': nrm(ks[4], (L, DEC_BATCH, N_MEM, MEM_HEADS, MEM_HD), DEEPNORM_BETA),
        'state_lru_conv': nrm(ks[5], (L, DEC_BATCH, LRU_CONV - 1, D_LRU), 1.0),
        'state_lru_h': nrm(ks[6], (L, DEC_BATCH, D_LRU), 0.5),
        'state_sc_conv': nrm(ks[7], (L, DEC_BATCH, SC_CONV - 1, D_SC), 1.0),
        'w_in': nrm(ks[8], (L, D_MODEL, D_IN), D_MODEL ** -0.5),
        'lru_conv_w': nrm(ks[9], (L, LRU_CONV, D_LRU), LRU_CONV ** -0.5),
        'lru_conv_b': nrm(ks[11], (L, D_LRU), 0.01),
        'w_rg_a': nrm(ks[12], (L, LRU_HEADS, LRU_HD, LRU_HD), LRU_HD ** -0.5),
        'b_rg_a': nrm(ks[15], (L, D_LRU), 0.01),
        'w_rg_x': nrm(ks[16], (L, LRU_HEADS, LRU_HD, LRU_HD), LRU_HD ** -0.5),
        'b_rg_x': nrm(ks[17], (L, D_LRU), 0.01),
        'lru_lambda': lam,
        'sc_conv_w': nrm(ks[18], (L, SC_CONV, D_SC), SC_CONV ** -0.5),
        'w_mem_kv': jnp.concatenate([w_k, w_v], axis=-1),
        'g_lru': 1.0 + nrm(ks[19], (L, D_LRU), 0.02),
        'g_sc': 1.0 + nrm(ks[20], (L, D_SC), 0.02),
        'g_mem': 1.0 + nrm(ks[21], (L, D_MEM), 0.02),
        'w_out': nrm(ks[22], (L, D_MIX, D_MODEL), DEEPNORM_BETA * D_MIX ** -0.5),
        'ln1_g': 1.0 + nrm(ks[23], (L, D_MODEL), 0.02),
        'ln1_b': nrm(ks[24], (L, D_MODEL), 0.02),
        'peer_wq': nrm(ks[25], (L, D_MODEL, PEER_HEADS * PEER_DK), D_MODEL ** -0.5),
        'peer_keys': nrm(ks[26], (L, PEER_HEADS, 2, N_KEYS, PEER_DK // 2), (PEER_DK // 2) ** -0.5),
        'peer_u': nrm(ks[27], (L, N_EXPERTS, D_MODEL), D_MODEL ** -0.5),
        'peer_v': nrm(ks[28], (L, N_EXPERTS, D_MODEL), DEEPNORM_BETA),
        'ln2_g': 1.0 + nrm(ks[29], (L, D_MODEL), 0.02),
        'ln2_b': nrm(ks[30], (L, D_MODEL), 0.02),
    }

def reference(x_prompt, x_sample, mem_prompt, cache_mem_k, cache_mem_v, state_lru_conv, state_lru_h,
              state_sc_conv, w_in, lru_conv_w, lru_conv_b, w_rg_a, b_rg_a, w_rg_x, b_rg_x, lru_lambda,
              sc_conv_w, w_mem_kv, g_lru, g_sc, g_mem, w_out, ln1_g, ln1_b, peer_wq, peer_keys, peer_u,
              peer_v, ln2_g, ln2_b):
    xp, xs = x_prompt, x_sample
    bsz = x_prompt.shape[0]
    mk_p, mv_p, lc_p, lh_p, sc_p, lc_s, lh_s, sc_s = [], [], [], [], [], [], [], []
    for l in range(DEPTH):
        lp = {'w_in': w_in[l], 'lru_conv_w': lru_conv_w[l], 'lru_conv_b': lru_conv_b[l],
              'w_rg_a': w_rg_a[l], 'b_rg_a': b_rg_a[l], 'w_rg_x': w_rg_x[l], 'b_rg_x': b_rg_x[l],
              'lru_lambda': lru_lambda[l], 'sc_conv_w': sc_conv_w[l], 'g_lru': g_lru[l], 'g_sc': g_sc[l],
              'g_mem': g_mem[l], 'w_out': w_out[l], 'ln1_g': ln1_g[l], 'ln1_b': ln1_b[l],
              'peer_wq': peer_wq[l], 'peer_keys': peer_keys[l], 'peer_u': peer_u[l], 'peer_v': peer_v[l],
              'ln2_g': ln2_g[l], 'ln2_b': ln2_b[l]}
        mk, mv = _mem_kv(mem_prompt, w_mem_kv[l])
        xp, nb, nh, ns = _layer(xp, mk, mv,
                                jnp.zeros((bsz, LRU_CONV - 1, D_LRU), xp.dtype),
                                jnp.zeros((bsz, D_LRU), jnp.float32),
                                jnp.zeros((bsz, SC_CONV - 1, D_SC), xp.dtype), lp)
        mk_p.append(mk); mv_p.append(mv); lc_p.append(nb); lh_p.append(nh); sc_p.append(ns)
        xs, nb, nh, ns = _layer(xs, cache_mem_k[l], cache_mem_v[l], state_lru_conv[l], state_lru_h[l],
                                state_sc_conv[l], lp)
        lc_s.append(nb); lh_s.append(nh); sc_s.append(ns)
    mem_k_prompt = jnp.stack(mk_p)
    mem_v_prompt = jnp.stack(mv_p)
    lru_conv_prompt = jnp.stack(lc_p)
    lru_h_prompt = jnp.stack(lh_p)
    sc_conv_prompt = jnp.stack(sc_p)
    lru_conv_sample = jnp.stack(lc_s)
    lru_h_sample = jnp.stack(lh_s)
    sc_conv_sample = jnp.stack(sc_s)
    return (xp, xs, mem_k_prompt, mem_v_prompt, lru_conv_prompt, lru_h_prompt, sc_conv_prompt,
            lru_conv_sample, lru_h_sample, sc_conv_sample)


_drawn_inputs = setup_inputs


def setup_inputs(seed=0):
    import zlib

    import numpy as np

    out = dict(_drawn_inputs(seed))
    spreads = {}
    factors = {'b_rg_a': 21.987,
     'b_rg_x': 6.535,
     'g_sc': 3.08,
     'g_mem': 3.0,
     'ln2_g': 8.544,
     'ln2_b': 8.103,
     'g_lru': 3.064}
    for name, (base, spread) in spreads.items():
        noise = np.random.default_rng([zlib.crc32(name.encode()), seed]).standard_normal(out[name].shape)
        drawn = base * np.exp(spread * noise) if base else spread * noise
        out[name] = __import__('jax').numpy.asarray(drawn.astype(out[name].dtype))
    for name, factor in factors.items():
        out[name] = (out[name] * factor).astype(out[name].dtype)
    return out
```

```python
import numpy as np
import concourse.bass as bass
from concourse import mybir

F32 = mybir.dt.float32
U32 = mybir.dt.uint32
ALU = mybir.AluOpType
ACT = mybir.ActivationFunctionType
AX = mybir.AxisListType

P = 128
D = 1024
KD = D // P
SEQ, SB, SS = 1024, 8, 8
NS = SB * SS
NT = SEQ + NS
NTD = NT + NS
BLOCKS = [(0, 512), (512, 512), (1024, 64)]
D_LRU, D_SC, D_MEM = 512, 256, 256
CL, CS, CM = D_LRU // P, D_SC // P, D_MEM // P
HD, MH, NM = 64, 4, 256
MC = NM // P
LRU_CONV, SC_CONV = 4, 3
PH, DK, NK, TOPK = 8, 128, 128, 16
SIDES = 2 * PH
SLOTS = PH * TOPK
TILES = SEQ // P
GRP = TOPK
RING = 8
DIAGS = 4
ALPHA = 2.0 ** 0.25
LN_EPS, RMS_EPS = 1e-5, 1e-6
LRU_C = 8.0
LOW = -3.0e38

PARAMS = [("conv_w", LRU_CONV * CL), ("conv_b", CL), ("b_a", CL), ("b_x", CL), ("lam", CL),
          ("sc_w", SC_CONV * CS), ("g", CL + CS + CM), ("h0", CL * SB)]
PCOL, NPAR = {}, 0
for _n, _w in PARAMS:
    PCOL[_n] = NPAR
    NPAR += _w
STATES = [("conv_p", CL * 3), ("h_p", CL), ("sc_p", CS * 2), ("conv_s", CL * SB * 3), ("h_s", CL * SB),
          ("sc_s", CS * SB * 2)]
SCOL, NST = {}, 0
for _n, _w in STATES:
    SCOL[_n] = NST
    NST += _w


class Carver:

    def __init__(self, arena, at):
        self.arena, self.at = arena, at

    def take(self, cols):
        a = self.arena[:, self.at:self.at + cols]
        self.at += cols
        return a


class Chain:

    def __init__(self, eng, sem):
        self.eng, self.sem, self.n = eng, sem, 0

    def did(self, ins):
        ins.then_inc(self.sem, 1)
        self.n += 1
        return self.n

    def wait(self):
        self.eng.wait_ge(self.sem, self.n)

    def link(self, ins):
        self.did(ins)
        self.wait()

    def restart(self):
        self.eng.sem_clear(self.sem)
        self.n = 0


def build(nc, A, O):
    ctx = []

    def sem(name):
        s = nc.semaphore(name)
        ctx.append(s)
        return s.__enter__()

    def sb(name, shape, dt=F32):
        t = nc.sbuf_tensor(name, shape, dt)
        ctx.append(t)
        return t.__enter__()

    ARENA = 50432
    arena_t = sb("arena", [P, ARENA])
    arena = arena_t[:, :]
    w = Carver(arena, 0)
    xT = w.take(KD * NT).rearrange("p (k t) -> p k t", k=KD)
    win = [w.take(KD * P).rearrange("p (k m) -> p k m", k=KD) for _ in range(4)]
    qT = w.take(CM * NT).rearrange("p (c t) -> p c t", c=CM)
    kT = w.take(CM * NM).rearrange("p (c m) -> p c m", c=CM)
    w = Carver(arena, 0)
    wq = w.take(SIDES * KD * DK)
    r = Carver(arena, w.at)
    yT = r.take((CL + CS + CM) * NTD).rearrange("p (c t) -> p c t", t=NTD)
    m = Carver(arena, r.at)
    w_out = r.take(KD * D).rearrange("p (k n) -> p k n", k=KD)
    memT = m.take(KD * NM).rearrange("p (k t) -> p k t", k=KD)
    wkv = m.take(KD * 2 * D_MEM).rearrange("p (k n) -> p k n", k=KD)
    ring = [arena[:, w.at + i * 2 * D:w.at + (i + 1) * 2 * D] for i in range(RING)]
    b = Carver(arena, r.at)
    kvp = b.take(MC * 2 * D_MEM)
    kv_v = kvp.rearrange("p (m n) -> p m n", m=MC)
    wrg = b.take(CL * 2 * P)
    wrg_v = wrg.rearrange("p (c g m) -> p c g m", c=CL, g=2)
    rmsb = b.take(NT)
    a = Carver(arena, b.at)
    rb, ib, db, ab, qb, sq = (b.take(NT) for _ in range(6))
    xl = b.take(3 + SEQ + SB * (3 + SS))
    xc = [b.take(NT) for _ in range(2)]
    gg = [b.take(NT) for _ in range(2)]
    scx = b.take(NT)
    scb, scc = xc[0], gg[0]
    cx = xl[:, 0:2 + SEQ + SB * (2 + SS)]
    ckT = a.take(SB * CM * NM).rearrange("p (b c m) -> p b c m", b=SB, c=CM)
    cv = a.take(SB * MC * D_MEM).rearrange("p (b c n) -> p b c n", b=SB, c=MC)
    prob = [a.take(MH * NM) for _ in range(2)]
    probT = [a.take(MH * NM) for _ in range(2)]
    st_s = a.take(2 * NM)
    c = Carver(arena, r.at)
    ln = c.take(4 * D)
    ln_v = ln.rearrange("p (i n) -> p i n", i=4)
    keysT = c.take(SIDES * NK)
    n = Carver(arena, c.at)
    xt = [n.take(D) for _ in range(2)]
    x1o = [n.take(D) for _ in range(2)]
    x1To = [n.take(D) for _ in range(2)]
    wst = [c.take(KD * DK) for _ in range(2)]
    x1c = c.take(D)
    x1n = c.take(D)
    x1Tn = c.take(D).rearrange("p (k t) -> p k t", k=KD)
    junk = [c.take(D) for _ in range(2)]
    diag = [c.take(P) for _ in range(DIAGS)]
    qTs = [c.take(P) for _ in range(2)]
    cand = [c.take(TOPK * TOPK) for _ in range(2)]
    onehot = c.take(TOPK * TOPK)
    sk1, sk2 = c.take(NK), c.take(NK)
    yout = c.take(D)
    assert max(x.at for x in (r, a, b, c, n)) <= ARENA, [x.at for x in (r, a, b, c, n)]

    consts = sb("consts", [P, 3 * P + TOPK])
    ident, fold, ones = (consts[:, i * P:(i + 1) * P] for i in range(3))
    iota16 = consts[:, 3 * P:3 * P + TOPK]
    par = sb("par", [P, NPAR])
    hb = sb("hb", [P, 8 * CL])
    st = sb("st", [P, NST])
    scst = sb("scst", [P, CS * SB * 2])
    cvst = sb("cvst", [P, CL * SB * 3])
    zero = sb("zero", [P, P])
    small = sb("small", [P, 64])
    eps = sb("eps", [P, 2])
    bst = sb("bst", [P, 12])
    mv = sb("mv", [P, 4])
    val = sb("val", [P, 2 * TOPK])
    idx = sb("idx", [P, 2 * TOPK], U32)
    idxf = sb("idxf", [P, 2 * TOPK])
    top = sb("top", [P, TOPK])
    ci = sb("ci", [P, TOPK], U32)
    ch = sb("ch", [P, 2 * TOPK], U32)
    ef = sb("ef", [P, 2 * TOPK])
    eu = sb("eu", [P, TOPK], U32)
    idx_w = sb("idx_w", [P, 2 * SLOTS], U32)
    sc_n = sb("sc_n", [P, SLOTS])
    ga_c = sb("ga_c", [P, SLOTS])
    ex = sb("ex", [P, SLOTS])
    den = sb("den", [P, 2 * PH])
    ibuf = [sb(f"ibuf{i}", [P, RING], U32) for i in range(2)]
    gbuf = sb("gbuf", [P, GRP])
    acts = sb("acts", [P, GRP])
    gel = sb("gel", [P, GRP])

    pt = nc.psum_tensor("ps", [P, 8 * 512], F32)
    ctx.append(pt)
    ps = pt.__enter__()
    bank = [ps[:, i * 512:(i + 1) * 512] for i in range(8)]

    ld = {k: sem("ld_" + k) for k in ("consts", "par", "cvst", "scst", "wrg", "memT", "wkv", "ln", "ckT", "cv",
                                      "wout", "wq", "keys", "x1T", "x1")}
    ld_xT = [sem(f"ld_xT{i}") for i in range(3)]
    ld_win = [sem(f"ld_win{i}") for i in range(4)]
    ld_xt = [sem(f"ld_xt{i}") for i in range(2)]
    st_kv, st_state, st_y = sem("st_kv"), sem("st_state"), sem("st_y")
    st_x1 = [sem(f"st_x1_{i}") for i in range(2)]
    st_x1T = [sem(f"st_x1T_{i}") for i in range(2)]
    proj_done, evac_done = sem("proj_done"), sem("evac_done")
    kv_done, kv_copied, kt_done, kt_copied = sem("kv_done"), sem("kv_copied"), sem("kt_done"), sem("kt_copied")
    conv_done, gate_mm, gate_ev, tau_done = sem("conv_done"), sem("gate_mm"), sem("gate_ev"), sem("tau_done")
    q_ready, root_done, y_done, sq_done = sem("q_ready"), sem("root_done"), sem("y_done"), sem("sq_done")
    rms_mm, rms_root, rms_done, prep_done, uexp_done = (sem("rms_mm"), sem("rms_root"), sem("rms_done"),
                                                        sem("prep_done"), sem("uexp_done"))
    s_mm, s_max, s_exp, s_norm, t_mm, t_copied, pv_mm, ym_done = (
        sem("s_mm"), sem("s_max"), sem("s_exp"), sem("s_norm"), sem("t_mm"), sem("t_copied"), sem("pv_mm"),
        sem("ym_done"))
    stt_mm, stt_cp, att_done = sem("stt_mm"), sem("stt_cp"), sem("att_done")
    op_mm, z_done, var_done, sd_done, x1_done, xt_mm, xt_cp = (
        sem("op_mm"), sem("z_done"), sem("var_done"), sem("sd_done"), sem("x1_done"), sem("xt_mm"), sem("xt_cp"))
    dve_c, turned, pe_zero = sem("dve_chain"), sem("turned"), sem("pe_zero")
    w_staged, w_used, qt_mm, qt_cp, sk_mm, sk_used = (sem("w_staged"), sem("w_used"), sem("qt_mm"), sem("qt_cp"),
                                                      sem("sk_mm"), sem("sk_used"))
    g_exp_in, g_exp, idx_ready = sem("g_exp_in"), sem("g_exp"), sem("idx_ready")
    gath = [sem(f"gath{i}") for i in range(RING)]
    dots, gelus, diags, used, y_mm, y_free, x1c_free, x1c_ready = (
        sem("dots"), sem("gelus"), sem("diags"), sem("used"), sem("y_mm"), sem("y_free"), sem("x1c_free"),
        sem("x1c_ready"))
    yo_ready, yo_free, v2_done, sd2_done = sem("yo_ready"), sem("yo_free"), sem("v2_done"), sem("sd2_done")

    def pcol(name, i):
        return par[:, PCOL[name] + i:PCOL[name] + i + 1]

    UNITS = [("lru", i, [i, CL + i]) for i in range(CL)] + \
            [("sc", i, [2 * CL + i, 2 * CL + CS + i, 2 * CL + 2 * CS + i]) for i in range(CS)] + \
            [("q", 0, [2 * CL + 3 * CS, 2 * CL + 3 * CS + 1])]
    MORDER = [mm for _, _, ms in UNITS for mm in ms]
    JOB0 = [3 * sum(len(x[2]) for x in UNITS[:k]) for k in range(len(UNITS) + 1)]
    NU = len(UNITS)
    AT = TILES + 1
    NL = TILES + 1

    def seg(buf, halo):
        return buf[:, 0:halo + SEQ], buf[:, halo + SEQ:].rearrange("p (s t) -> p s t", s=SB)

    xlp, xls = seg(xl, 3)
    cxp, cxs = seg(cx, 2)

    def tok(buf):
        return buf[:, 0:SEQ], buf[:, SEQ:NT].rearrange("p (s t) -> p s t", s=SB)

    block = nc.Block()
    ctx.append(block)
    block = block.__enter__()

    @block.sync
    def _(sp):
        def load(name, dst, src):
            sp.dma_start(dst, src).then_inc(ld[name] if isinstance(name, str) else name, 16)

        load("consts", consts[:, :], A["consts"])
        load("par", par[:, :], A["par"])
        load("memT", memT, A["memT"])
        load("wkv", wkv, A["wkv"])
        for i in range(4):
            load(ld_win[i], win[i], A["w_in"][MORDER[i]])
            if i < 3:
                t0, tn = BLOCKS[i]
                load(ld_xT[i], xT[:, :, t0:t0 + tn], A["xT"][:, :, t0:t0 + tn])
        load("cvst", cvst[:, :], A["cvst"])
        load("scst", scst[:, :], A["scst"])
        load("wrg", wrg, A["wrg"])
        sp.wait_ge(kv_copied, MC)
        for c_ in range(MC):
            sp.dma_start(O["kv"][c_ * P:(c_ + 1) * P, :], kv_v[:, c_, :]).then_inc(st_kv, 16)
        load("wout", w_out, A["w_out"])
        for i in range(4, len(MORDER)):
            sp.wait_ge(proj_done, 3 * (i - 3))
            load(ld_win[i % 4], win[i % 4], A["w_in"][MORDER[i]])
        sp.wait_ge(y_done, CL + CS)
        sp.wait_ge(sq_done, CL + CS)
        sp.wait_ge(rms_mm, CL + CS)
        load("ckT", ckT, A["ckT"])
        load("cv", cv, A["cv"])
        sp.wait_ge(att_done, 1)
        sp.wait_ge(st_kv, 16 * MC)
        load("ln", ln_v, A["ln"].partition_broadcast(P))
        sp.dma_start(O["states"], st[:, :]).then_inc(st_state, 16)
        load(ld_xt[0], xt[0], A["x_tok"][0])
        load(ld_xt[1], xt[1], A["x_tok"][1])
        load("wq", wq, A["wq"])
        load("keys", keysT, A["keys"])
        for t in range(NL):
            sp.wait_ge(x1_done, t + 1)
            sp.dma_start(O["x1"][t * P:(t + 1) * P, :], x1o[t % 2]).then_inc(st_x1[t % 2], 16)
            if t + 2 < NL:
                load(ld_xt[t % 2], xt[t % 2], A["x_tok"][t + 2])
            sp.wait_ge(xt_cp, t + 1)
            sp.dma_start(O["x1T"][t * P:(t + 1) * P, :], x1To[t % 2]).then_inc(st_x1T[t % 2], 16)
        for i in range(2):
            cnt = len(range(i, NL, 2))
            sp.wait_ge(st_x1[i], 16 * cnt)
            sp.wait_ge(st_x1T[i], 16 * cnt)

        def x1T_of(row):
            return O["x1T"][bass.ds(row, P), :].rearrange("p (k t) -> p k t", k=KD)

        load("x1T", x1Tn, x1T_of(0))
        load("x1", x1n, O["x1"][0:P, :])
        sp.wait_ge(st_state, 16)
        sp.nop().then_inc(yo_free, 1)
        with sp.Fori(0, TILES) as tau:
            sp.wait_ge(qt_mm, (tau + 1) * SIDES + 2)
            load("x1T", x1Tn, x1T_of((tau + 1) * P))
            sp.wait_ge(x1c_ready, tau + 1)
            load("x1", x1n, O["x1"][bass.ds((tau + 1) * P, P), :])
            sp.wait_ge(yo_ready, tau + 1)
            sp.dma_start(O["y"][bass.ds(tau * P, P), :], yout).then_inc(st_y, 16)
            sp.wait_ge(st_y, 16 * (tau + 1))
            sp.nop().then_inc(yo_free, 1)
        sp.wait_ge(yo_ready, TILES + 1)
        sp.dma_start(O["y"][TILES * P:, :], yout).then_inc(st_y, 16)
        sp.wait_ge(st_y, 16 * (TILES + 1))

    @block.gpsimd
    def _(pool):
        def turn(turn_no):
            first = turn_no * GRP
            for half in range(2):
                pool.wait_ge(idx_ready, 2 * turn_no + half + 1)
                pool.sem_inc(turned, 1)
                for i in range(RING):
                    s = half * RING + i
                    pool.wait_ge(used, first + s + 1)
                    pool.sem_inc(turned, 1)
                    pool.indirect_dma_start(
                        out=ring[i], out_offset=None, in_=A["uv"],
                        in_offset=bass.IndirectOffsetOnAxis(ap=ibuf[half][:, i:i + 1], axis=0)).then_inc(gath[i], 16)

        with pool.Fori(0, TILES) as tau:
            with pool.Fori(0, PH) as h:
                turn(tau * PH + h)
        with pool.Fori(0, PH // 2) as h:
            turn(h + TILES * PH)

    @block.tensor
    def _(pe):
        mm = nc.tensor.matmul

        pe.wait_ge(ld["consts"], 16)
        pe.wait_ge(ld["memT"], 16)
        pe.wait_ge(ld["wkv"], 16)
        for c_ in range(MC):
            for k in range(KD):
                last = mm(bank[c_], memT[:, k, c_ * P:(c_ + 1) * P], wkv[:, k, :], start=k == 0, stop=k == KD - 1)
            last.then_inc(kv_done, 1)
        for e in range(CM):
            for c_ in range(MC):
                pe.wait_ge(kv_copied, c_ + 1)
                last = nc.tensor.transpose(bank[2 + e][:, c_ * P:(c_ + 1) * P], kv_v[:, c_, e * P:(e + 1) * P], ident)
            last.then_inc(kt_done, 1)
        pe.wait_ge(kt_copied, CM)

        def project(k):
            job = JOB0[k]
            for mm_ in UNITS[k][2]:
                i = MORDER.index(mm_)
                pe.wait_ge(ld_win[i % 4], 16 * (i // 4 + 1))
                for bi, (t0, tn) in enumerate(BLOCKS):
                    if i == 0:
                        pe.wait_ge(ld_xT[bi], 16)
                    if job >= 3:
                        pe.wait_ge(evac_done, job - 2)
                    for kk in range(KD):
                        last = mm(bank[job % 3][:, 0:tn], win[i % 4][:, kk, :], xT[:, kk, t0:t0 + tn],
                                  start=kk == 0, stop=kk == KD - 1)
                    last.then_inc(proj_done, 1)
                    job += 1

        def gates(c_):
            if c_ == 0:
                pe.wait_ge(ld["wrg"], 16)
            pe.wait_ge(conv_done, c_ + 1)
            for bi, (t0, tn) in enumerate(BLOCKS):
                for g in range(2):
                    job = (c_ * 3 + bi) * 2 + g
                    if job >= 2:
                        pe.wait_ge(gate_ev, job - 1)
                    mm(bank[3 + g][:, 0:tn], wrg_v[:, c_, g, :], xc[c_ % 2][:, t0:t0 + tn], start=True, stop=True)\
                        .then_inc(gate_mm, 1)

        def sumsq(k, first, last_, group):
            pe.wait_ge(sq_done, k + 1)
            if first and group:
                pe.wait_ge(rms_root, group)
            for bi, (t0, tn) in enumerate(BLOCKS):
                l_ = mm(bank[5 + bi][:, 0:tn], ones, sq[:, t0:t0 + tn], start=first, stop=last_)
            l_.then_inc(rms_mm, 1)

        for k in range(NU):
            project(k)
            if 1 <= k <= CL:
                gates(k - 1)
            if 2 <= k:
                sumsq(k - 2, k - 2 in (0, CL), k - 2 in (CL - 1, CL + CS - 1), int(k - 2 >= CL))
        sumsq(CL + CS - 1, False, True, 1)

        def transposes(t, heads):
            pe.wait_ge(s_norm, t + 1)
            if t >= 1:
                pe.wait_ge(t_copied, t)
            for j in range(heads * MC):
                last = nc.tensor.transpose(ps[:, 1024 + j * P:1024 + (j + 1) * P], prob[t % 2][:, j * P:(j + 1) * P],
                                           ident)
            last.then_inc(t_mm, 1)

        def scores(t):
            if t == 0:
                pe.wait_ge(evac_done, JOB0[NU])
            if t >= 1:
                pe.wait_ge(s_exp, t)
            for h in range(MH):
                lo = HD * (h % 2)
                j = (h % 2) * 2 + h // 2
                last = mm(ps[:, j * NM:(j + 1) * NM], qT[lo:lo + HD, h // 2, t * P:(t + 1) * P],
                          kT[lo:lo + HD, h // 2, :], start=True, stop=True)
            last.then_inc(s_mm, 1)

        def values(t):
            pe.wait_ge(t_copied, t + 1)
            if t >= 1:
                pe.wait_ge(ym_done, t)
            pv = probT[t % 2].rearrange("p (h c t) -> p h c t", h=MH, c=MC)
            for h in range(MH):
                lo = HD * (h % 2)
                for c_ in range(MC):
                    last = mm(bank[4][lo:lo + HD, (h // 2) * P:(h // 2) * P + P],
                              kv_v[:, c_, D_MEM + h * HD:D_MEM + (h + 1) * HD], pv[:, (h % 2) * 2 + h // 2, c_, :],
                              start=c_ == 0, stop=c_ == MC - 1)
            last.then_inc(pv_mm, 1)

        scores(0)
        for t in range(TILES):
            transposes(t, MH)
            if t + 1 < TILES:
                scores(t + 1)
            values(t)
        t = TILES
        pe.wait_ge(s_exp, t)
        pe.wait_ge(ld["ckT"], 16)
        sT = [bank[g][:, 0:NM].rearrange("p (c h b t) -> p c h b t", c=MC, h=2, b=SB) for g in range(2)]
        for c_ in range(MC):
            for h in range(MH):
                lo = HD * (h % 2)
                for b_ in range(SB):
                    q0 = SEQ + b_ * SS
                    last = mm(sT[h % 2][:, c_, h // 2, b_, :], ckT[lo:lo + HD, b_, h // 2, c_ * P:(c_ + 1) * P],
                              qT[lo:lo + HD, h // 2, q0:q0 + SS], start=True, stop=True)
        last.then_inc(stt_mm, 1)
        pe.wait_ge(stt_cp, 1)
        pe.wait_ge(rms_root, 2)
        stv = st_s.rearrange("p (g c t) -> p g c t", c=MC, g=2)
        for g in range(2):
            for c_ in range(MC):
                last = nc.tensor.transpose(bank[5][:, (g * MC + c_) * P:(g * MC + c_ + 1) * P], stv[:, g, c_, :], ident)
        last.then_inc(s_mm, 1)
        transposes(t, 2)
        pe.wait_ge(t_copied, t + 1)
        pe.wait_ge(ym_done, t)
        pe.wait_ge(ld["cv"], 16)
        pv = probT[t % 2].rearrange("p (g c h b t) -> p g c h b t", g=4, c=MC, h=2, b=SB)
        for h in range(MH):
            lo = HD * (h % 2)
            for b_ in range(SB):
                for c_ in range(MC):
                    o0 = (h // 2) * NS + b_ * SS
                    last = mm(bank[4][lo:lo + HD, o0:o0 + SS], cv[:, b_, c_, h * HD:(h + 1) * HD],
                              pv[:, h % 2, c_, h // 2, b_, :], start=c_ == 0, stop=c_ == MC - 1)
        last.then_inc(pv_mm, 1)
        for k in range(CM):
            sumsq(CL + CS + k, k == 0, k == CM - 1, 2)

        pe.wait_ge(ld["wout"], 16)
        pe.wait_ge(rms_done, 3)

        def turn_x1(t):
            pe.wait_ge(x1_done, t + 1)
            if t >= 1:
                pe.wait_ge(xt_cp, t)
            for k in range(KD):
                last = nc.tensor.transpose(ps[:, 2048 + k * P:2048 + (k + 1) * P], x1o[t % 2][:, k * P:(k + 1) * P],
                                           ident)
            last.then_inc(xt_mm, 1)

        for t in range(NL):
            if t >= 2:
                pe.wait_ge(z_done, t - 1)
            if t == TILES:
                pe.wait_ge(att_done, 1)
            for k in range(KD):
                for hf in range(2):
                    last = mm(bank[(t % 2) * 2 + hf], yT[:, k, t * P:(t + 1) * P],
                              w_out[:, k, hf * 512:(hf + 1) * 512], start=k == 0, stop=k == KD - 1)
            last.then_inc(op_mm, 1)
            if t >= 1:
                turn_x1(t - 1)
        turn_x1(NL - 1)

        def query(side, piece, tile):
            if side == 0:
                pe.wait_ge(ld["x1T"], 16 * (tile + 1))
            pe.wait_ge(w_staged, piece + 1)
            pe.wait_ge(qt_cp, piece + 1)
            for k in range(KD):
                last = mm(bank[2][:, 0:P], wst[side][:, k * P:(k + 1) * P], x1Tn[:, k, :], start=k == 0,
                          stop=k == KD - 1)
            last.then_inc(qt_mm, 1)

        def keyscore(side, piece, col):
            pe.wait_ge(qt_cp, piece + 2)
            pe.wait_ge(sk_used, piece + 1)
            mm(bank[3][:, 0:NK], qTs[side], keysT[:, bass.ds(col, NK)], start=True, stop=True).then_inc(sk_mm, 1)

        def turn(turn_no, tile=None, h=None):
            first = turn_no * GRP
            for s in range(GRP):
                pe.wait_ge(diags, first + s + 2)
                pe.wait_ge(gath[s % RING], turn_no * (16 * GRP // RING) + 16 * (s // RING + 1))
                v = ring[s % RING][:, D:2 * D]
                for hf in range(2):
                    last = mm(bank[hf], diag[s % DIAGS], v[:, hf * 512:(hf + 1) * 512], start=False, stop=False)
                last.then_inc(used, 1)
                if tile is None:
                    continue
                if s in (4, 10):
                    query(int(s == 10), tile * SIDES + h * 2 + int(s == 10), tile)
                if s in (8, 14):
                    keyscore(int(s == 14), tile * SIDES + h * 2 + int(s == 14), h * (2 * NK) + int(s == 14) * NK)

        def open_y(tile):
            pe.wait_ge(y_free, tile + 1)
            for hf in range(2):
                mm(bank[hf], zero[:, :], ln[:, hf * 512:(hf + 1) * 512], start=True, stop=False)

        def close_y():
            for hf in range(2):
                last = mm(bank[hf], zero[:, :], ln[:, hf * 512:(hf + 1) * 512], start=False, stop=True)
            last.then_inc(y_mm, 1)

        pe.wait_ge(pe_zero, 1)
        pe.wait_ge(ld["keys"], 16)
        pe.wait_ge(ld["ln"], 16)
        pe.nop().then_inc(qt_mm, 2)
        pe.nop().then_inc(sk_mm, 2)
        pe.wait_ge(ld["x1T"], 16)
        pe.nop().then_inc(used, RING)
        with pe.Fori(0, PH) as h:
            query(0, h * 2, 0)
            keyscore(0, h * 2, h * (2 * NK))
            query(1, h * 2 + 1, 0)
            keyscore(1, h * 2 + 1, h * (2 * NK) + NK)
        with pe.Fori(0, TILES) as tau:
            open_y(tau)
            with pe.Fori(0, PH) as h:
                turn(tau * PH + h, tau + 1, h)
            close_y()
        open_y(TILES)
        with pe.Fori(0, PH // 2) as h:
            turn(h + TILES * PH)
        close_y()

    @block.scalar
    def _(act):
        A_ = nc.scalar.activation
        act.wait_ge(prep_done, 1)
        A_(hb[:, CL:2 * CL], hb[:, 0:CL], ACT.Exp).then_inc(uexp_done, 1)

        def evac(k):
            kind, c_, ms = UNITS[k]
            job = JOB0[k]
            for j in range(len(ms)):
                for bi, (t0, tn) in enumerate(BLOCKS):
                    act.wait_ge(proj_done, job + 1)
                    src = bank[job % 3][:, 0:tn]
                    if bi == 0:
                        if kind == "lru" and j == 0 and k >= 1:
                            act.wait_ge(conv_done, k)
                        if kind == "lru" and j == 1 and k >= 2:
                            act.wait_ge(y_done, k - 1)
                        if kind == "sc" and j == 0:
                            act.wait_ge(y_done, k - 1 + c_)
                    if kind == "lru" and j == 0:
                        dst = xlp[:, 3 + t0:3 + t0 + tn] if bi < 2 else xls[:, :, 3:]
                    elif kind == "lru":
                        dst = gg[c_ % 2][:, t0:t0 + tn]
                    elif kind == "sc":
                        dst = (scb, scc, scx)[j][:, t0:t0 + tn]
                    else:
                        dst = qT[:, j, t0:t0 + tn]
                    if kind == "lru" and j == 0 and bi == 2:
                        src = src.rearrange("p (s t) -> p s t", s=SB)
                    A_(dst, src, ACT.Gelu if kind == "lru" and j else ACT.Copy).then_inc(evac_done, 1)
                    job += 1

        def square(k, src):
            if k >= 1:
                act.wait_ge(rms_mm, k)
            A_(sq, src, ACT.Square).then_inc(sq_done, 1)

        def post_gates(c_):
            if c_ >= 1:
                act.wait_ge(y_done, c_)
            for bi, (t0, tn) in enumerate(BLOCKS):
                for g, (dst, bias) in enumerate(((rb, "b_a"), (ib, "b_x"))):
                    act.wait_ge(gate_mm, (c_ * 3 + bi) * 2 + g + 1)
                    A_(dst[:, t0:t0 + tn], bank[3 + g][:, 0:tn], ACT.Sigmoid, bias=pcol(bias, c_)).then_inc(gate_ev, 1)
            act.wait_ge(gate_ev, (c_ + 1) * 6)
            if c_ == 0:
                act.wait_ge(prep_done, 2)
            A_(rb, rb, ACT.Tanh, scale=hb[:, 7 * CL + c_:7 * CL + c_ + 1]).then_inc(tau_done, 1)
            act.wait_ge(q_ready, c_ + 1)
            A_(qb, qb, ACT.Sqrt, scale=-1.0).then_inc(root_done, 1)

        def rms(group, width):
            done = (CL, CL + CS, CL + CS + CM)[group]
            act.wait_ge(rms_mm, done)
            for bi, (t0, tn) in enumerate(BLOCKS):
                last = A_(rmsb[:, t0:t0 + tn], bank[5 + bi][:, 0:tn], ACT.Sqrt, scale=1.0 / width, bias=eps[:, 0:1])
            last.then_inc(rms_root, 1)

        act.wait_ge(kt_done, CM)
        for e in range(CM):
            A_(kT[:, e, :], bank[2 + e][:, 0:NM], ACT.Copy).then_inc(kt_copied, 1)
        act.wait_ge(ld["par"], 16)
        for k in range(NU):
            evac(k)
            if 1 <= k <= CL:
                post_gates(k - 1)
            if 2 <= k:
                act.wait_ge(y_done, k - 1)
                square(k - 2, yT[:, k - 2, 0:NT])
            if k == NU - 1:
                rms(0, D_LRU)
        act.wait_ge(y_done, CL + CS)
        square(CL + CS - 1, yT[:, CL + CS - 1, 0:NT])
        act.wait_ge(rms_done, 1)
        rms(1, D_SC)

        def attend(t, heads, base):
            act.wait_ge(s_max, t + 1)
            if t >= 2:
                act.wait_ge(t_mm, t - 1)
            for h in range(heads):
                last = A_(prob[t % 2][:, h * NM:(h + 1) * NM], ps[:, base + h * NM:base + (h + 1) * NM], ACT.Exp,
                          scale=HD ** -0.5, bias=small[:, (t % 2) * 16 + 4 + h:(t % 2) * 16 + 5 + h],
                          accum_out=small[:, (t % 2) * 16 + 8 + h:(t % 2) * 16 + 9 + h])
            last.then_inc(s_exp, 1)

        def copyT(t, heads):
            act.wait_ge(t_mm, t + 1)
            if t >= 2:
                act.wait_ge(pv_mm, t - 1)
            A_(probT[t % 2][:, 0:heads * NM], ps[:, 1024:1024 + heads * NM], ACT.Copy).then_inc(t_copied, 1)

        act.wait_ge(rms_done, 2)
        for t in range(TILES):
            attend(t, MH, 0)
            if t >= 1:
                copyT(t - 1, MH)
        copyT(TILES - 1, MH)
        act.wait_ge(stt_mm, 1)
        A_(st_s.rearrange("p (g n) -> p g n", g=2), ps[:, 0:D].rearrange("p (g n) -> p g n", g=2)[:, :, 0:NM], ACT.Copy).then_inc(stt_cp, 1)
        attend(TILES, 2, 5 * 512)
        copyT(TILES, 2)
        act.wait_ge(ym_done, AT)
        for k in range(CM):
            square(CL + CS + k, yT[:, CL + CS + k, 0:NT])
        rms(2, D_MEM)

        def dev(t):
            act.wait_ge(var_done, t + 1)
            A_(mv[:, 2:3], mv[:, 1:2], ACT.Sqrt, bias=eps[:, 1:2]).then_inc(sd_done, 1)

        def copy_x1T(t):
            act.wait_ge(xt_mm, t + 1)
            if t >= 2:
                act.wait_ge(st_x1T[t % 2], 16 * (t // 2))
            A_(x1To[t % 2], ps[:, 2048:2048 + D], ACT.Copy).then_inc(xt_cp, 1)

        for t in range(NL):
            dev(t)
            if t >= 1:
                copy_x1T(t - 1)
        copy_x1T(NL - 1)

        def stage(side, piece, h):
            act.wait_ge(qt_mm, piece + 1)
            A_(wst[side], wq[:, bass.ds(h * (2 * KD * DK) + side * (KD * DK), KD * DK)], ACT.Copy)\
                .then_inc(w_staged, 1)

        def copy_q(side, piece):
            act.wait_ge(qt_mm, piece + 3)
            act.wait_ge(sk_mm, piece + 1)
            A_(qTs[side], bank[2][:, 0:P], ACT.Copy).then_inc(qt_cp, 1)

        act.wait_ge(ld["wq"], 16)
        act.wait_ge(ld["x1"], 16)
        act.nop().then_inc(qt_cp, 1)

        def turn(turn_no, piece=None, h=None):
            first = turn_no * GRP
            for s in range(GRP):
                act.wait_ge(dots, first + s + 1)
                if s == 0:
                    act.wait_ge(diags, first + 1)
                A_(gel[:, s:s + 1], acts[:, s:s + 1], ACT.Gelu).then_inc(gelus, 1)
                if piece is not None:
                    if s in (1, 8):
                        stage(int(s == 8), piece + int(s == 8), h)
                    if s in (7, 13):
                        copy_q(int(s == 13), piece + int(s == 13))

        def gates_exp(tile):
            act.wait_ge(g_exp_in, tile + 1)
            A_(ex[:, :], ex[:, :], ACT.Exp).then_inc(g_exp, 1)

        def next_x1(tile):
            act.wait_ge(ld["x1"], 16 * (tile + 1))
            act.wait_ge(x1c_free, tile + 1)
            A_(x1c, x1n, ACT.Copy).then_inc(x1c_ready, 1)

        def dev2(tile):
            act.wait_ge(v2_done, tile + 1)
            A_(mv[:, 2:3], mv[:, 1:2], ACT.Sqrt, bias=eps[:, 1:2]).then_inc(sd2_done, 1)

        with act.Fori(0, PH) as h:
            for side in range(2):
                stage(side, h * 2 + side, h)
                copy_q(side, h * 2 + side)
        gates_exp(0)
        next_x1(0)
        with act.Fori(0, TILES) as tau:
            with act.Fori(0, PH) as h:
                turn(tau * PH + h, (tau + 1) * SIDES + h * 2, h)
            gates_exp(tau + 1)
            next_x1(tau + 1)
            dev2(tau)
        with act.Fori(0, PH // 2) as h:
            turn(h + TILES * PH)
        dev2(TILES)

    @block.vector
    def _(dve):
        V = nc.vector
        chain = Chain(dve, dve_c)
        link, did = chain.link, chain.did
        did(V.memset(eps[:, 0:1], RMS_EPS))
        did(V.memset(eps[:, 1:2], LN_EPS))
        V.memset(zero[:, :], 0.0).then_inc(pe_zero, 1)
        chain.wait()
        dve.wait_ge(ld["par"], 16)
        lam = par[:, PCOL["lam"]:PCOL["lam"] + CL]
        H = [hb[:, i * CL:(i + 1) * CL] for i in range(8)]
        V.scalar_tensor_tensor(H[0], lam, -1.0, lam, ALU.mult, ALU.min).then_inc(prep_done, 1)
        dve.wait_ge(uexp_done, 1)
        link(V.tensor_scalar(H[2], H[1], 2.0, None, ALU.add))
        link(V.reciprocal(H[3], H[2]))
        link(V.tensor_tensor(H[2], H[1], H[3], ALU.mult))
        link(V.tensor_tensor(H[3], H[2], H[2], ALU.mult))
        link(V.tensor_scalar(H[4], H[3], 1.0 / 17, 1.0 / 15, ALU.mult, ALU.add))
        for j in (13, 11, 9, 7, 5, 3, 1):
            link(V.tensor_tensor(H[5], H[4], H[3], ALU.mult))
            link(V.tensor_scalar(H[4], H[5], 1.0 / j, None, ALU.add))
        link(V.tensor_tensor(H[5], H[4], H[2], ALU.mult))
        link(V.tensor_scalar(H[6], lam, -LRU_C / 2, 0.0, ALU.mult, ALU.max))
        V.scalar_tensor_tensor(H[7], H[5], LRU_C, H[6], ALU.mult, ALU.add).then_inc(prep_done, 1)
        for c_ in range(MC):
            dve.wait_ge(kv_done, c_ + 1)
            V.tensor_copy(kv_v[:, c_, :], bank[c_]).then_inc(kv_copied, 1)
        dve.wait_ge(ld["cvst"], 16)
        dve.wait_ge(ld["scst"], 16)
        did(V.memset(xlp[:, 0:3], 0.0))
        chain.wait()

        def save(name, width, c_, src, n_):
            dst = st[:, SCOL[name] + c_ * width:SCOL[name] + (c_ + 1) * width]
            if n_:
                dst = dst.rearrange("p (s t) -> p s t", s=SB)
            return V.tensor_copy(dst, src)

        def taps(out_, buf, halo, w_name, c_, bias):
            for j in range(halo + 1):
                wj = pcol(w_name, c_ * (halo + 1) + j)
                for o_, b_, n_ in ((tok(out_)[0], seg(buf, halo)[0], SEQ), (tok(out_)[1], seg(buf, halo)[1], SS)):
                    x_ = b_[:, j:j + n_] if n_ == SEQ else b_[:, :, j:j + n_]
                    if j == 0:
                        if bias is None:
                            did(V.tensor_scalar(o_, x_, wj, None, ALU.mult))
                        else:
                            did(V.tensor_scalar(o_, x_, wj, bias, ALU.mult, ALU.add))
                    else:
                        last = did(V.scalar_tensor_tensor(o_, x_, wj, o_, ALU.mult, ALU.add))
                chain.wait()

        def conv(k):
            c_ = k
            did(V.tensor_copy(xls[:, :, 0:3], cvst[:, c_ * SB * 3:(c_ + 1) * SB * 3].rearrange("p (s t) -> p s t", s=SB)))
            chain.wait()
            dve.wait_ge(evac_done, JOB0[k] + 3)
            did(save("conv_p", 3, c_, xlp[:, SEQ:SEQ + 3], 0))
            did(save("conv_s", SB * 3, c_, xls[:, :, SS:SS + 3], 1))
            if k >= 2:
                dve.wait_ge(y_done, k - 1)
                dve.wait_ge(gate_mm, (k - 1) * 6)
            taps(xc[c_ % 2], xl, 3, "conv_w", c_, pcol("conv_b", c_))
            dve.nop().then_inc(conv_done, 1)

        def recur(c_):
            dve.wait_ge(tau_done, c_ + 1)
            link(V.tensor_scalar(db, rb, 1.0, None, ALU.add))
            link(V.reciprocal(ab, db))
            link(V.scalar_tensor_tensor(db, rb, 2.0, ab, ALU.mult, ALU.mult))
            did(V.tensor_scalar(ab, db, -1.0, 1.0, ALU.mult, ALU.add))
            V.scalar_tensor_tensor(qb, db, 2.0, db, ALU.subtract, ALU.mult).then_inc(q_ready, 1)
            chain.wait()
            dve.wait_ge(gate_ev, (c_ + 1) * 6)
            link(V.tensor_tensor(ib, ib, xc[c_ % 2], ALU.mult))
            dve.wait_ge(root_done, c_ + 1)
            link(V.tensor_tensor(ib, ib, qb, ALU.mult))
            a0 = tok(ab)[1][:, :, 0]
            b0 = tok(ib)[1][:, :, 0]
            tmp = small[:, 32:32 + SB]
            link(V.tensor_tensor(tmp, a0, par[:, PCOL["h0"] + c_ * SB:PCOL["h0"] + (c_ + 1) * SB], ALU.mult))
            did(V.tensor_tensor(b0, b0, tmp, ALU.add))
            did(V.memset(a0, 0.0))
            chain.wait()
            link(V.tensor_tensor_scan(db, ab, ib, 0.0, ALU.mult, ALU.add))
            did(save("h_p", 1, c_, db[:, SEQ - 1:SEQ], 0))
            did(V.tensor_copy(st[:, SCOL["h_s"] + c_ * SB:SCOL["h_s"] + (c_ + 1) * SB], tok(db)[1][:, :, SS - 1]))
            dve.wait_ge(evac_done, JOB0[c_] + 6)
            link(V.tensor_tensor(yT[:, c_, 0:NT], db, gg[c_ % 2], ALU.mult))
            dve.nop().then_inc(y_done, 1)

        def short_conv(k):
            c_ = UNITS[k][1]
            if c_ == 0:
                did(V.memset(cxp[:, 0:2], 0.0))
            did(V.tensor_copy(cxs[:, :, 0:2], scst[:, c_ * SB * 2:(c_ + 1) * SB * 2].rearrange("p (s t) -> p s t", s=SB)))
            dve.wait_ge(evac_done, JOB0[k] + 9)
            did(V.tensor_tensor(cxp[:, 2:], tok(scc)[0], tok(scx)[0], ALU.mult))
            did(V.tensor_tensor(cxs[:, :, 2:], tok(scc)[1], tok(scx)[1], ALU.mult))
            chain.wait()
            did(save("sc_p", 2, c_, cxp[:, SEQ:SEQ + 2], 0))
            did(save("sc_s", SB * 2, c_, cxs[:, :, SS:SS + 2], 1))
            taps(yT[:, CL + c_, 0:NT], cx, 2, "sc_w", c_, None)
            link(V.tensor_tensor(yT[:, CL + c_, 0:NT], yT[:, CL + c_, 0:NT], scb, ALU.mult))
            dve.nop().then_inc(y_done, 1)

        def norm(group, lo, hi):
            dve.wait_ge(rms_root, group + 1)
            link(V.reciprocal(rmsb, rmsb))
            for k in range(lo, hi):
                did(V.scalar_tensor_tensor(yT[:, k, 0:NT], yT[:, k, 0:NT], pcol("g", k), rmsb, ALU.mult, ALU.mult))
            chain.wait()
            dve.nop().then_inc(rms_done, 1)

        for k in range(NU):
            if k < CL:
                conv(k)
            if 1 <= k <= CL:
                recur(k - 1)
            if UNITS[k][0] == "sc":
                short_conv(k)
        dve.wait_ge(sq_done, CL + CS)
        norm(0, 0, CL)
        norm(1, CL, CL + CS)

        def biases(t, heads, base):
            o = (t % 2) * 16
            dve.wait_ge(s_mm, t + 1)
            if t >= 2:
                dve.wait_ge(s_norm, t - 1)
            link(V.tensor_reduce(small[:, o:o + heads],
                                 ps[:, base:base + heads * NM].rearrange("p (h m) -> p h m", h=heads), AX.X, ALU.max))
            V.tensor_scalar(small[:, o + 4:o + 4 + heads], small[:, o:o + heads], -HD ** -0.5, None, ALU.mult)\
                .then_inc(s_max, 1)

        def normalize(t, heads):
            o = (t % 2) * 16
            dve.wait_ge(s_exp, t + 1)
            link(V.reciprocal(small[:, o + 12:o + 12 + heads], small[:, o + 8:o + 8 + heads]))
            for h in range(heads):
                pr = prob[t % 2][:, h * NM:(h + 1) * NM]
                did(V.tensor_scalar(pr, pr, small[:, o + 12 + h:o + 13 + h], None, ALU.mult))
            chain.wait()
            dve.nop().then_inc(s_norm, 1)

        def take_y(t):
            dve.wait_ge(pv_mm, t + 1)
            w_ = P if t < TILES else NS
            V.tensor_copy(yT[:, CL + CS:, t * P:t * P + w_],
                          bank[4][:, 0:CM * w_].rearrange("p (c t) -> p c t", c=CM)).then_inc(ym_done, 1)

        for t in range(TILES):
            biases(t, MH, 0)
            normalize(t, MH)
            if t >= 1:
                take_y(t - 1)
        take_y(TILES - 1)
        biases(TILES, 2, 5 * 512)
        normalize(TILES, 2)
        take_y(TILES)
        norm(2, CL + CS, CL + CS + CM)
        link(V.tensor_copy(yT[:, :, NT:NTD], yT[:, :, SEQ:NT]))
        dve.nop().then_inc(rms_done, 1)
        dve.nop().then_inc(att_done, 1)

        def layernorm(x_, psum, z, dst, gi, var_sem, sd_sem, tile, zsem):
            ins = V.scalar_tensor_tensor(z, x_, ALPHA, psum, ALU.mult, ALU.add)
            link(ins)
            dve.nop().then_inc(zsem, 1)
            for hf in range(2):
                did(V.bn_stats(bst[:, hf * 6:(hf + 1) * 6], z[:, hf * 512:(hf + 1) * 512]))
            chain.wait()
            link(V.bn_aggr(mv[:, 0:2], bst[:, :]))
            dve.nop().then_inc(var_sem, 1)
            dve.wait_ge(sd_sem, tile + 1)
            link(V.reciprocal(mv[:, 3:4], mv[:, 2:3]))
            link(V.tensor_scalar(z, z, mv[:, 0:1], mv[:, 3:4], ALU.subtract, ALU.mult))
            link(V.tensor_tensor(z, z, ln_v[:, gi, :], ALU.mult))
            link(V.tensor_tensor(dst, z, ln_v[:, gi + 1, :], ALU.add))

        dve.wait_ge(ld["ln"], 16)
        for t in range(NL):
            dve.wait_ge(op_mm, t + 1)
            dve.wait_ge(ld_xt[t % 2], 16 * (t // 2 + 1))
            if t >= 2:
                dve.wait_ge(st_x1[t % 2], 16 * (t // 2))
                dve.wait_ge(xt_mm, t - 1)
            layernorm(xt[t % 2], ps[:, (t % 2) * D:(t % 2 + 1) * D], x1o[t % 2], x1o[t % 2], 0, var_done, sd_done, t,
                      z_done)
            dve.nop().then_inc(x1_done, 1)

        dve.wait_ge(ld["x1"], 16)
        for s_ in (sk_used, x1c_free, y_free, diags):
            dve.nop().then_inc(s_, 1)

        def top16(scr, src, vals, inds):
            link(V.max(vals[:, 0:8], src))
            did(V.max_index(inds[:, 0:8], vals[:, 0:8], src))
            link(V.match_replace(scr, vals[:, 0:8], src, LOW))
            link(V.max(vals[:, 8:16], scr))
            link(V.max_index(inds[:, 8:16], vals[:, 8:16], scr))

        def side_top(side, piece):
            dve.wait_ge(sk_mm, piece + 3)
            link(V.tensor_copy(sk1, bank[3][:, 0:NK]))
            dve.nop().then_inc(sk_used, 1)
            top16(sk2, sk1, val[:, side * TOPK:(side + 1) * TOPK], idx[:, side * TOPK:(side + 1) * TOPK])

        def b3(ap, inner):
            return (ap.unsqueeze(2) if inner else ap.unsqueeze(1)).broadcast_to([P, TOPK, TOPK])

        def head_top(h):
            v3 = cand[0].rearrange("p (i j) -> p i j", i=TOPK)
            oh = onehot.rearrange("p (i j) -> p i j", i=TOPK)
            did(V.tensor_copy(idxf[:, :], idx[:, :]))
            link(V.tensor_tensor(v3, b3(val[:, 0:TOPK], True), b3(val[:, TOPK:], False), ALU.add))
            top16(cand[1], cand[0], top, ci)
            did(V.tensor_scalar(ch[:, 0:TOPK], ci[:, :], 4, None, ALU.logical_shift_right))
            did(V.tensor_scalar(ch[:, TOPK:], ci[:, :], TOPK - 1, None, ALU.bitwise_and))
            chain.wait()
            for sd in range(2):
                link(V.tensor_tensor(oh, b3(ch[:, sd * TOPK:(sd + 1) * TOPK], True), b3(iota16, False), ALU.is_equal))
                link(V.tensor_tensor(oh, oh, b3(idxf[:, sd * TOPK:(sd + 1) * TOPK], False), ALU.mult))
                link(V.tensor_reduce(ef[:, sd * TOPK:(sd + 1) * TOPK], oh, AX.X, ALU.add))
            link(V.scalar_tensor_tensor(eu[:, :], ef[:, 0:TOPK], float(NK), ef[:, TOPK:], ALU.mult, ALU.add))
            for lo, hh in ((0, h), (P // 2, (h + PH // 2) % PH)):
                did(V.tensor_copy(idx_w[lo:lo + P // 2, bass.ds(hh * TOPK + SLOTS, TOPK)], eu[lo:lo + P // 2, :]))
                did(V.tensor_copy(sc_n[lo:lo + P // 2, bass.ds(hh * TOPK, TOPK)], top[lo:lo + P // 2, :]))
            chain.wait()

        def promote(tile):
            s3 = sc_n[:, :].rearrange("p (h k) -> p h k", h=PH)
            e3 = ex[:, :].rearrange("p (h k) -> p h k", h=PH)
            did(V.tensor_copy(idx_w[:, 0:SLOTS], idx_w[:, SLOTS:]))
            link(V.tensor_tensor(e3, s3, s3[:, :, 0:1].broadcast_to([P, PH, TOPK]), ALU.subtract))
            dve.nop().then_inc(g_exp_in, 1)
            dve.wait_ge(g_exp, tile + 1)
            link(V.tensor_reduce(den[:, 0:PH], e3, AX.X, ALU.add))
            link(V.reciprocal(den[:, PH:], den[:, 0:PH]))
            link(V.tensor_tensor(ga_c[:, :].rearrange("p (h k) -> p h k", h=PH), e3,
                                 den[:, PH:].unsqueeze(2).broadcast_to([P, PH, TOPK]), ALU.mult))

        def put_diag(first, s, sel):
            dve.wait_ge(gelus, first + s + 1)
            dve.wait_ge(used, first + s + 1 + RING - DIAGS)
            V.tensor_scalar(diag[s % DIAGS], sel, gel[:, s:s + 1], gbuf[:, s:s + 1], ALU.mult, ALU.mult)\
                .then_inc(diags, 1)

        def turn(turn_no, tile, sel, h, piece=None):
            first = turn_no * GRP
            V.tensor_copy(ibuf[1][:, :], idx_w[:, bass.ds(h * GRP + RING, RING)]).then_inc(idx_ready, 1)
            dve.wait_ge(diags, first + 1)
            link(V.tensor_copy(gbuf[:, :], ga_c[:, bass.ds(h * GRP, GRP)]))
            dve.wait_ge(x1c_ready, tile + 1)
            for s in range(GRP):
                dve.wait_ge(gath[s % RING], turn_no * (16 * GRP // RING) + 16 * (s // RING + 1))
                V.tensor_tensor_reduce(out=junk[s % 2], in0=ring[s % RING][:, 0:D], in1=x1c, scale=1.0, scalar=0.0,
                                       op0=ALU.mult, op1=ALU.add, accum_out=acts[:, s:s + 1]).then_inc(dots, 1)
                if s >= 1:
                    put_diag(first, s - 1, sel)
                if s == RING - 1:
                    V.tensor_copy(ibuf[0][:, :], idx_w[:, bass.ds(h * GRP + GRP, RING)]).then_inc(idx_ready, 1)
                if piece is not None and s == 10:
                    side_top(0, piece)
            put_diag(first, GRP - 1, sel)
            if piece is not None:
                side_top(1, piece + 1)
                head_top(h)

        def finish(tile):
            dve.wait_ge(y_mm, tile + 1)
            dve.wait_ge(yo_free, tile + 1)
            link(V.scalar_tensor_tensor(yout, x1c, ALPHA, ps[:, 0:D], ALU.mult, ALU.add))
            dve.nop().then_inc(y_free, 1)
            dve.nop().then_inc(x1c_free, 1)
            for hf in range(2):
                did(V.bn_stats(bst[:, hf * 6:(hf + 1) * 6], yout[:, hf * 512:(hf + 1) * 512]))
            chain.wait()
            link(V.bn_aggr(mv[:, 0:2], bst[:, :]))
            dve.nop().then_inc(v2_done, 1)
            dve.wait_ge(sd2_done, tile + 1)
            link(V.reciprocal(mv[:, 3:4], mv[:, 2:3]))
            link(V.tensor_scalar(yout, yout, mv[:, 0:1], mv[:, 3:4], ALU.subtract, ALU.mult))
            link(V.tensor_tensor(yout, yout, ln_v[:, 2, :], ALU.mult))
            link(V.tensor_tensor(yout, yout, ln_v[:, 3, :], ALU.add))
            dve.nop().then_inc(yo_ready, 1)

        chain.wait()
        with dve.Fori(0, PH) as h:
            chain.restart()
            side_top(0, h * 2)
            side_top(1, h * 2 + 1)
            head_top(h)
        chain.restart()
        promote(0)
        V.tensor_copy(ibuf[0][:, :], idx_w[:, 0:RING]).then_inc(idx_ready, 1)
        with dve.Fori(0, TILES) as tau:
            with dve.Fori(0, PH) as h:
                chain.restart()
                turn(tau * PH + h, tau, ident, h, (tau + 1) * SIDES + h * 2)
            chain.restart()
            promote(tau + 1)
            finish(tau)
        with dve.Fori(0, PH // 2) as h:
            chain.restart()
            turn(h + TILES * PH, TILES, fold, h)
        chain.restart()
        finish(TILES)

    for x in reversed(ctx):
        x.__exit__(None, None, None)


INPUTS = ["consts", "par", "cvst", "scst", "wrg", "memT", "wkv", "w_in", "xT", "w_out", "ln", "ckT", "cv", "x_tok",
          "wq", "keys", "uv"]


def kernel(**inp):
    import concourse.bacc as bacc
    from concourse.bass_utils import run_bass_kernel_spmd

    i = {k: np.asarray(v) for k, v in inp.items()}

    def cols(v, n):
        v = v.reshape(-1, n, P)
        return np.ascontiguousarray(v.transpose(2, 1, 0).reshape(P, -1))

    xs = i["x_sample"].reshape(NS, D)
    x_tok = np.concatenate([i["x_prompt"][0], xs, xs])
    xT = np.concatenate([i["x_prompt"][0], xs]).T

    def by_k(m):
        return np.ascontiguousarray(m.reshape(-1, P, m.shape[1]).transpose(1, 0, 2))

    wrg = np.zeros((P, CL, 2, P), np.float32)
    for g, name in enumerate(("w_rg_a", "w_rg_x")):
        for h in range(2 * CL):
            lo = HD * (h % 2)
            wrg[lo:lo + HD, h // 2, g, lo:lo + HD] = i[name][0, h]
    par = np.concatenate([
        cols(i["lru_conv_w"][0], CL), cols(i["lru_conv_b"][0], CL), cols(i["b_rg_a"][0], CL),
        cols(i["b_rg_x"][0], CL), cols(i["lru_lambda"][0], CL), cols(i["sc_conv_w"][0], CS),
        cols(i["g_lru"][0], CL), cols(i["g_sc"][0], CS), cols(i["g_mem"][0], CM),
        cols(i["state_lru_h"][0], CL)], axis=1)
    half = np.arange(P) % NS
    consts = np.concatenate([np.eye(P), half[:, None] == half[None, :], np.ones((P, P)),
                             np.tile(np.arange(TOPK), (P, 1))], axis=1).astype(np.float32)
    w_in = i["w_in"][0].reshape(KD, P, -1, P).transpose(2, 1, 0, 3)
    ck = i["cache_mem_k"][0].reshape(SB, NM, CM, P).transpose(3, 0, 2, 1)
    cv = i["cache_mem_v"][0].reshape(SB, MC, P, D_MEM).transpose(2, 0, 1, 3)
    wq = i["peer_wq"][0].reshape(KD, P, SIDES, DK).transpose(1, 2, 0, 3)
    keys = i["peer_keys"][0].reshape(SIDES, NK, DK).transpose(2, 0, 1)
    arrays = {
        "consts": consts, "par": par, "cvst": cols(i["state_lru_conv"][0], CL),
        "scst": cols(i["state_sc_conv"][0], CS), "wrg": wrg.reshape(P, -1),
        "memT": by_k(i["mem_prompt"][0].T), "wkv": by_k(i["w_mem_kv"][0]), "w_in": w_in, "xT": by_k(xT),
        "w_out": by_k(i["w_out"][0]),
        "ln": np.stack([i["ln1_g"][0], i["ln1_b"][0], i["ln2_g"][0], i["ln2_b"][0]]),
        "ckT": ck, "cv": cv, "x_tok": x_tok.reshape(TILES + 1, P, D),
        "wq": wq.reshape(P, -1), "keys": keys.reshape(P, -1),
        "uv": np.concatenate([i["peer_u"][0], i["peer_v"][0]], axis=1),
    }
    nc = bacc.Bacc("TRN2", target_bir_lowering=False, num_devices=1)
    A, feeds = {}, {}
    for name in INPUTS:
        arr = np.ascontiguousarray(arrays[name], dtype=np.float32)
        feeds["in_" + name] = arr
        A[name] = nc.dram_tensor("in_" + name, arr.shape, F32, kind="ExternalInput").ap()
    O = {}
    for name, shape in (("kv", (NM, 2 * D_MEM)), ("states", (P, NST)), ("y", ((TILES + 1) * P, D))):
        O[name] = nc.dram_tensor("out_" + name, shape, F32, kind="ExternalOutput").ap()
    for name in ("x1", "x1T"):
        O[name] = nc.dram_tensor("scratch_" + name, ((TILES + 1) * P, D), F32).ap()
    build(nc, A, O)
    r = run_bass_kernel_spmd(nc, [feeds], core_ids=[0]).results[0]
    y, kv, st = r["out_y"], r["out_kv"], r["out_states"]

    def state(name, n, *rest):
        w = n * int(np.prod(rest, dtype=int))
        v = st[:, SCOL[name]:SCOL[name] + w].reshape(P, n, *rest)
        axes = list(range(2, 2 + len(rest))) + [1, 0]
        return np.ascontiguousarray(v.transpose(axes)).reshape(*rest, n * P)

    return (
        y[:SEQ].reshape(1, SEQ, D), y[SEQ:SEQ + NS].reshape(SB, SS, D),
        kv[:, :D_MEM].reshape(1, 1, NM, MH, HD), kv[:, D_MEM:].reshape(1, 1, NM, MH, HD),
        state("conv_p", CL, 3)[None, None], state("h_p", CL, 1)[None], state("sc_p", CS, 2)[None, None],
        state("conv_s", CL, SB, 3)[None], state("h_s", CL, SB)[None], state("sc_s", CS, SB, 2)[None])
```

```python
import numpy as np
import concourse.bass as bass
from concourse import mybir

F32 = mybir.dt.float32
U32 = mybir.dt.uint32
ALU = mybir.AluOpType
ACT = mybir.ActivationFunctionType
AX = mybir.AxisListType

P = 128
D = 1024
KD = D // P
SEQ, SB, SS = 1024, 8, 8
NS = SB * SS
NT = SEQ + NS
NTD = NT + NS
BLOCKS = [(0, 384), (384, 384), (768, 320)]
LASTP = SEQ - 768
D_LRU, D_SC, D_MEM = 512, 256, 256
CL, CS, CM = D_LRU // P, D_SC // P, D_MEM // P
HD, MH, NM = 64, 4, 256
MC = NM // P
LRU_CONV, SC_CONV = 4, 3
PH, DK, NK, TOPK = 8, 128, 128, 16
SIDES = 2 * PH
SLOTS = PH * TOPK
TILES = SEQ // P
GRP = TOPK
RING = 8
DIAGS = 4
WIN = 3
ALPHA = 2.0 ** 0.25
LN_EPS, RMS_EPS = 1e-5, 1e-6
LRU_C = 8.0
LOW = -3.0e38

PARAMS = [("conv_w", LRU_CONV * CL), ("conv_b", CL), ("b_a", CL), ("b_x", CL), ("lam", CL),
          ("sc_w", SC_CONV * CS), ("g", CL + CS + CM), ("h0", CL * SB)]
PCOL, NPAR = {}, 0
for _n, _w in PARAMS:
    PCOL[_n] = NPAR
    NPAR += _w
STATES = [("conv_p", CL * 3), ("h_p", CL), ("sc_p", CS * 2), ("conv_s", CL * SB * 3), ("h_s", CL * SB),
          ("sc_s", CS * SB * 2)]
SCOL, NST = {}, 0
for _n, _w in STATES:
    SCOL[_n] = NST
    NST += _w


class Carver:

    def __init__(self, arena, at):
        self.arena, self.at = arena, at

    def take(self, cols):
        a = self.arena[:, self.at:self.at + cols]
        self.at += cols
        return a


class Chain:

    def __init__(self, eng, sem):
        self.eng, self.sem, self.n = eng, sem, 0

    def did(self, ins):
        ins.then_inc(self.sem, 1)
        self.n += 1
        return self.n

    def wait(self):
        self.eng.wait_ge(self.sem, self.n)

    def link(self, ins):
        self.did(ins)
        self.wait()

    def restart(self):
        self.eng.sem_clear(self.sem)
        self.n = 0


def build(nc, A, O):
    ctx = []

    def sem(name):
        s = nc.semaphore(name)
        ctx.append(s)
        return s.__enter__()

    def sb(name, shape, dt=F32):
        t = nc.sbuf_tensor(name, shape, dt)
        ctx.append(t)
        return t.__enter__()

    ARENA = 50560
    arena_t = sb("arena", [P, ARENA])
    arena = arena_t[:, :]
    w = Carver(arena, 0)
    xT = w.take(KD * NT).rearrange("p (k t) -> p k t", k=KD)
    win = [w.take(KD * P).rearrange("p (k m) -> p k m", k=KD) for _ in range(WIN)]
    qT = w.take(CM * NT).rearrange("p (c t) -> p c t", c=CM)
    kT = w.take(CM * NM).rearrange("p (c m) -> p c m", c=CM)
    scx1 = arena[:, w.at:w.at + NT]
    prob = [w.take(2 * NM) for _ in range(2)]
    probT0 = w.take(2 * NM)
    assert w.at <= SIDES * KD * DK
    w = Carver(arena, 0)
    wq = w.take(SIDES * KD * DK)
    r = Carver(arena, w.at)
    yT = r.take((CL + CS + CM) * NTD).rearrange("p (c t) -> p c t", t=NTD)
    m = Carver(arena, r.at)
    mc = Carver(arena, r.at)
    w_out = r.take(KD * D).rearrange("p (k n) -> p k n", k=KD)
    memT = m.take(KD * NM).rearrange("p (k t) -> p k t", k=KD)
    wkv = m.take(KD * 2 * D_MEM).rearrange("p (k n) -> p k n", k=KD)
    ckT = mc.take(SB * CM * NM).rearrange("p (b c m) -> p b c m", b=SB, c=CM)
    cv = mc.take(SB * MC * D_MEM).rearrange("p (b c n) -> p b c n", b=SB, c=MC)
    ring = [arena[:, w.at + i * 2 * D:w.at + (i + 1) * 2 * D] for i in range(RING)]
    b = Carver(arena, r.at)
    kvp = b.take(MC * 2 * D_MEM)
    kv_v = kvp.rearrange("p (m n) -> p m n", m=MC)
    wrg = b.take(CL * 2 * P)
    wrg_v = wrg.rearrange("p (c g m) -> p c g m", c=CL, g=2)
    rmsb = b.take(NT)
    rb, ib, db, ab, qb, sq = (b.take(NT) for _ in range(6))
    xl = b.take(3 + SEQ + SB * (3 + SS))
    xc = [b.take(NT) for _ in range(2)]
    gg = [b.take(NT) for _ in range(2)]
    scx = [b.take(NT), scx1]
    scb, scc = xc, gg
    cx = xl[:, 0:2 + SEQ + SB * (2 + SS)]
    probT = [probT0, b.take(2 * NM)]
    st_s = probT[1]
    q2 = rmsb[:, 0:CM * SB * 2 * SS].rearrange("p (c b g t) -> p c b g t", c=CM, b=SB, g=2)
    rmsbuf = [rmsb, rb, ib]
    c = Carver(arena, r.at)
    ln = c.take(4 * D)
    ln_v = ln.rearrange("p (i n) -> p i n", i=4)
    keysT = c.take(SIDES * NK)
    wst = [c.take(KD * DK) for _ in range(2)]
    qTs = [c.take(P) for _ in range(2)]
    cand = [c.take(TOPK * TOPK) for _ in range(2)]
    onehot = c.take(TOPK * TOPK)
    sk2 = c.take(NK)
    yout = c.take(D)
    x1T0 = yout.rearrange("p (k t) -> p k t", k=KD)
    n = Carver(arena, c.at)
    xt = [n.take(D) for _ in range(2)]
    x1o = [n.take(D) for _ in range(2)]
    x1To = [n.take(D) for _ in range(2)]
    x1c = c.take(D)
    x1n = c.take(D)
    x1Tn = c.take(D).rearrange("p (k t) -> p k t", k=KD)
    junk = [c.take(D) for _ in range(2)]
    diag = [c.take(P) for _ in range(DIAGS)]
    assert max(x.at for x in (r, b, c, n)) <= ARENA, [x.at for x in (r, b, c, n)]

    consts = sb("consts", [P, 3 * P + TOPK])
    ident, fold, ones = (consts[:, i * P:(i + 1) * P] for i in range(3))
    iota16 = consts[:, 3 * P:3 * P + TOPK]
    par = sb("par", [P, NPAR])
    hb = sb("hb", [P, 8 * CL])
    st = sb("st", [P, NST])
    scst = sb("scst", [P, CS * SB * 2])
    cvst = sb("cvst", [P, CL * SB * 3])
    zero = sb("zero", [P, P])
    small = sb("small", [P, 64])
    eps = sb("eps", [P, 2])
    bst = sb("bst", [P, 12])
    mv = sb("mv", [P, 4])
    val = sb("val", [P, 2 * TOPK])
    idx = sb("idx", [P, 2 * TOPK], U32)
    idxf = sb("idxf", [P, 2 * TOPK])
    top = sb("top", [P, TOPK])
    ci = sb("ci", [P, TOPK], U32)
    ch = sb("ch", [P, 2 * TOPK], U32)
    ef = sb("ef", [P, 2 * TOPK])
    eu = sb("eu", [P, TOPK], U32)
    idx_w = sb("idx_w", [P, 2 * SLOTS], U32)
    sc_n = sb("sc_n", [P, SLOTS])
    ga_c = sb("ga_c", [P, SLOTS])
    ex = sb("ex", [P, SLOTS])
    den = sb("den", [P, 2 * PH])
    ibuf = [sb(f"ibuf{i}", [P, RING], U32) for i in range(2)]
    gbuf = sb("gbuf", [P, GRP])
    acts = sb("acts", [P, GRP])
    gel = sb("gel", [P, GRP])
    wt = sb("wt", [P, GRP])

    pt = nc.psum_tensor("ps", [P, 8 * 512], F32)
    ctx.append(pt)
    ps = pt.__enter__()
    bank = [ps[:, i * 512:(i + 1) * 512] for i in range(8)]

    ld = {k: sem("ld_" + k) for k in ("consts", "par", "cvst", "scst", "wrg", "memT", "wkv", "ln", "ckT", "cv",
                                      "wout", "wq", "keys", "x1T0", "x1T", "x1")}
    ld_xT = [sem(f"ld_xT{i}") for i in range(3)]
    ld_win = [sem(f"ld_win{i}") for i in range(WIN)]
    ld_xt = [sem(f"ld_xt{i}") for i in range(2)]
    st_kv, st_state, st_y = sem("st_kv"), sem("st_state"), sem("st_y")
    st_x1 = [sem(f"st_x1_{i}") for i in range(2)]
    st_x1T = [sem(f"st_x1T_{i}") for i in range(2)]
    proj_done, evac_done = sem("proj_done"), sem("evac_done")
    kv_done, kv_copied, kt_done, kt_copied = sem("kv_done"), sem("kv_copied"), sem("kt_done"), sem("kt_copied")
    conv_done, gate_mm, gate_ev, tau_done = sem("conv_done"), sem("gate_mm"), sem("gate_ev"), sem("tau_done")
    q_ready, root_done, y_done, sq_done = sem("q_ready"), sem("root_done"), sem("y_done"), sem("sq_done")
    rms_mm, rms_root, norm_done, prep_done, uexp_done = (sem("rms_mm"), sem("rms_root"), sem("norm_done"),
                                                        sem("prep_done"), sem("uexp_done"))
    s_mm, s_max, s_exp, s_norm, t_mm, t_copied, pv_mm, ym_done = (
        sem("s_mm"), sem("s_max"), sem("s_exp"), sem("s_norm"), sem("t_mm"), sem("t_copied"), sem("pv_mm"),
        sem("ym_done"))
    q2_ready, stt_mm, stt_cp, mixer_done = sem("q2_ready"), sem("stt_mm"), sem("stt_cp"), sem("mixer_done")
    op_mm, z_done, var_done, sd_done, x1_done, xt_mm, xt_cp = (
        sem("op_mm"), sem("z_done"), sem("var_done"), sem("sd_done"), sem("x1_done"), sem("xt_mm"), sem("xt_cp"))
    dve_c, turned, dve_turned, pe_zero = sem("dve_chain"), sem("turned"), sem("dve_turned"), sem("pe_zero")
    w_staged, qt_mm, qt_cp, sk_mm, sk_used = (sem("w_staged"), sem("qt_mm"), sem("qt_cp"),
                                              sem("sk_mm"), sem("sk_used"))
    g_exp_in, g_exp, idx_ready = sem("g_exp_in"), sem("g_exp"), sem("idx_ready")
    gath = [sem(f"gath{i}") for i in range(RING)]
    gates_in, weights = sem("gates_in"), sem("weights")
    dots, gelus, diags, used, y_mm, y_free, x1c_free, x1c_ready = (
        sem("dots"), sem("gelus"), sem("diags"), sem("used"), sem("y_mm"), sem("y_free"), sem("x1c_free"),
        sem("x1c_ready"))
    yo_ready, yo_free, v2_done, sd2_done = sem("yo_ready"), sem("yo_free"), sem("v2_done"), sem("sd2_done")

    def pcol(name, i):
        return par[:, PCOL[name] + i:PCOL[name] + i + 1]

    UNITS = [("q", 0, [2 * CL + 3 * CS, 2 * CL + 3 * CS + 1])] + \
            [("lru", i, [i, CL + i]) for i in range(CL)] + \
            [("sc", i, [2 * CL + 2 * CS + i, 2 * CL + i, 2 * CL + CS + i]) for i in range(CS)]
    MORDER = [mm for _, _, ms in UNITS for mm in ms]
    JOB0 = [3 * sum(len(x[2]) for x in UNITS[:k]) for k in range(len(UNITS) + 1)]
    NU = len(UNITS)
    K_LRU, K_SC = 1, 1 + CL
    STEPS = 2 * TILES
    ROUNDS = STEPS + 6
    SUMS = [CL + CS + i for i in range(CM)] + list(range(CL + CS))
    GROUPS = [(0, CM, D_MEM), (CM, CM + CL, D_LRU), (CM + CL, CM + CL + CS, D_SC)]
    NL = TILES + 1

    def abank(j):
        return bank[5 + j % 3]

    def attention_round(job):
        n = job - JOB0[K_LRU]
        return n if 0 <= n < ROUNDS else None

    def seg(buf, halo):
        return buf[:, 0:halo + SEQ], buf[:, halo + SEQ:].rearrange("p (s t) -> p s t", s=SB)

    xlp, xls = seg(xl, 3)
    cxp, cxs = seg(cx, 2)

    def tok(buf):
        return buf[:, 0:SEQ], buf[:, SEQ:NT].rearrange("p (s t) -> p s t", s=SB)

    block = nc.Block()
    ctx.append(block)
    block = block.__enter__()

    ONE, EARLY, LATE = (0, 4), (0, 2), (7, 2)
    STAGE, QUERY, COPY_Q, KEYS, TOP = 0, 1, 3, 4, 6
    TAIL = 12

    def due(routes, s, step):
        return [(r_, side) for r_ in routes for side in range(2) if r_[3][0] + side * r_[3][1] + step == s]

    def tile0_turn(h):
        return [(h * 2 + 2, 0, h + 2, EARLY), (h * 2 + 3, 1, h, LATE)]

    def next_turn(tile, h):
        return [(tile * PH + h, tile, h, ONE)]

    LEAD = 2

    def all_turns(eng, turn, begin, end):
        begin(0)
        with eng.Fori(0, PH - LEAD) as h:
            turn(h, 0, h, tile0_turn(h))
        with eng.Fori(PH - LEAD, PH) as h:
            turn(h, 0, h, next_turn(1, h))
        end(0)
        with eng.Fori(1, TILES) as tau:
            begin(tau)
            turn(tau * PH, tau, 0, next_turn(tau + 1, 0), True)
            with eng.Fori(1, PH) as h:
                turn(tau * PH + h, tau, h, next_turn(tau + 1, h))
            end(tau)
        begin(TILES)
        turn(TILES * PH, TILES, 0, [], True)
        with eng.Fori(1, PH // 2) as h:
            turn(h + TILES * PH, TILES, h, [])
        end(TILES)

    @block.sync
    def _(sp):
        def load(name, dst, src):
            sp.dma_start(dst, src).then_inc(ld[name] if isinstance(name, str) else name, 16)

        load("consts", consts[:, :], A["consts"])
        load("par", par[:, :], A["par"])
        load("memT", memT, A["memT"])
        load("wkv", wkv, A["wkv"])
        for i in range(3):
            load(ld_win[i % WIN], win[i % WIN], A["w_in"][MORDER[i]])
            t0, tn = BLOCKS[i]
            load(ld_xT[i], xT[:, :, t0:t0 + tn], A["xT"][:, :, t0:t0 + tn])
        load("cvst", cvst[:, :], A["cvst"])
        load("scst", scst[:, :], A["scst"])
        load("wrg", wrg, A["wrg"])
        sp.wait_ge(kv_copied, MC)
        for c_ in range(MC):
            sp.dma_start(O["kv"][c_ * P:(c_ + 1) * P, :], kv_v[:, c_, :]).then_inc(st_kv, 16)
        load("ckT", ckT, A["ckT"])
        load("cv", cv, A["cv"])
        for i in range(WIN, len(MORDER)):
            sp.wait_ge(proj_done, 3 * (i - WIN + 1))
            load(ld_win[i % WIN], win[i % WIN], A["w_in"][MORDER[i]])
        sp.wait_ge(ym_done, STEPS + 1)
        load("wout", w_out, A["w_out"])
        sp.wait_ge(mixer_done, 1)
        sp.wait_ge(st_kv, 16 * MC)
        load("ln", ln_v, A["ln"].partition_broadcast(P))
        sp.dma_start(O["states"], st[:, :]).then_inc(st_state, 16)
        load(ld_xt[0], xt[0], A["x_tok"][0])
        load(ld_xt[1], xt[1], A["x_tok"][1])
        load("wq", wq, A["wq"])
        load("keys", keysT, A["keys"])
        for t in range(NL):
            sp.wait_ge(x1_done, t + 1)
            sp.dma_start(O["x1"][t * P:(t + 1) * P, :], x1o[t % 2]).then_inc(st_x1[t % 2], 16)
            if t + 2 < NL:
                load(ld_xt[t % 2], xt[t % 2], A["x_tok"][t + 2])
            sp.wait_ge(xt_cp, t + 1)
            sp.dma_start(O["x1T"][t * P:(t + 1) * P, :], x1To[t % 2]).then_inc(st_x1T[t % 2], 16)
            if t == 1:
                sp.wait_ge(st_x1T[0], 16)
                load("x1T0", x1T0, O["x1T"][0:P, :].rearrange("p (k t) -> p k t", k=KD))
        for i in range(2):
            cnt = len(range(i, NL, 2))
            sp.wait_ge(st_x1[i], 16 * cnt)
            sp.wait_ge(st_x1T[i], 16 * cnt)

        def x1T_of(row):
            return O["x1T"][bass.ds(row, P), :].rearrange("p (k t) -> p k t", k=KD)

        load("x1", x1n, O["x1"][0:P, :])
        load("x1T", x1Tn, x1T_of(P))
        sp.wait_ge(st_state, 16)
        sp.wait_ge(x1c_ready, 1)
        load("x1", x1n, O["x1"][P:2 * P, :])
        sp.nop().then_inc(yo_free, 1)
        with sp.Fori(1, TILES) as tau:
            sp.wait_ge(qt_mm, (tau + 1) * SIDES + 2)
            load("x1T", x1Tn, x1T_of((tau + 1) * P))
            sp.wait_ge(x1c_ready, tau + 1)
            load("x1", x1n, O["x1"][bass.ds((tau + 1) * P, P), :])
            sp.wait_ge(yo_ready, tau)
            sp.dma_start(O["y"][bass.ds(tau * P - P, P), :], yout).then_inc(st_y, 16)
            sp.wait_ge(st_y, tau * 16)
            sp.nop().then_inc(yo_free, 1)
        for t in (TILES - 1, TILES):
            sp.wait_ge(yo_ready, t + 1)
            sp.dma_start(O["y"][t * P:(t + 1) * P, :], yout).then_inc(st_y, 16)
            sp.wait_ge(st_y, 16 * (t + 1))
            sp.nop().then_inc(yo_free, 1)

    @block.gpsimd
    def _(pool):
        def turn(turn_no, tile, h, routes, tail=False):
            first = turn_no * GRP
            for half in range(2):
                pool.wait_ge(idx_ready, 2 * turn_no + half + 1)
                pool.sem_inc(turned, 1)
                for i in range(RING):
                    s = half * RING + i
                    pool.wait_ge(used, first + s + 1)
                    pool.sem_inc(turned, 1)
                    pool.indirect_dma_start(
                        out=ring[i], out_offset=None, in_=A["uv"],
                        in_offset=bass.IndirectOffsetOnAxis(ap=ibuf[half][:, i:i + 1], axis=0)).then_inc(gath[i], 16)

        pool.wait_ge(op_mm, NL)
        all_turns(pool, turn, lambda tile: None, lambda tile: None)

    def is_tile0(tile):
        return isinstance(tile, int) and tile == 0

    @block.tensor
    def _(pe):
        mm = nc.tensor.matmul

        pe.wait_ge(ld["consts"], 16)
        pe.wait_ge(ld["memT"], 16)
        pe.wait_ge(ld["wkv"], 16)
        for c_ in range(MC):
            for k in range(KD):
                last = mm(bank[c_], memT[:, k, c_ * P:(c_ + 1) * P], wkv[:, k, :], start=k == 0, stop=k == KD - 1)
            last.then_inc(kv_done, 1)
        for e in range(CM):
            for c_ in range(MC):
                pe.wait_ge(kv_copied, c_ + 1)
                last = nc.tensor.transpose(bank[2 + e][:, c_ * P:(c_ + 1) * P], kv_v[:, c_, e * P:(e + 1) * P], ident)
            last.then_inc(kt_done, 1)
        pe.wait_ge(kt_copied, CM)

        def project(k, after):
            job = JOB0[k]
            for mm_ in UNITS[k][2]:
                i = MORDER.index(mm_)
                pe.wait_ge(ld_win[i % WIN], 16 * (i // WIN + 1))
                for bi, (t0, tn) in enumerate(BLOCKS):
                    if i == 0:
                        pe.wait_ge(ld_xT[bi], 16)
                    if job >= 3:
                        pe.wait_ge(evac_done, job - 2)
                    for kk in range(KD):
                        last = mm(bank[job % 3][:, 0:tn], win[i % WIN][:, kk, :], xT[:, kk, t0:t0 + tn],
                                  start=kk == 0, stop=kk == KD - 1)
                    last.then_inc(proj_done, 1)
                    after(job)
                    job += 1

        def gates(c_):
            if c_ == 0:
                pe.wait_ge(ld["wrg"], 16)
            pe.wait_ge(conv_done, c_ + 1)
            for bi, (t0, tn) in enumerate(BLOCKS):
                for g in range(2):
                    job = (c_ * 3 + bi) * 2 + g
                    if job >= 2:
                        pe.wait_ge(gate_ev, job - 1)
                    mm(bank[3 + g][:, 0:tn], wrg_v[:, c_, g, :], xc[c_ % 2][:, t0:t0 + tn], start=True, stop=True)\
                        .then_inc(gate_mm, 1)

        def sumsq(n):
            group = [g for g in range(3) if GROUPS[g][0] <= n < GROUPS[g][1]][0]
            first, last_ = n == GROUPS[group][0], n == GROUPS[group][1] - 1
            pe.wait_ge(sq_done, n + 1)
            if first and group:
                pe.wait_ge(rms_root, group)
            for bi, (t0, tn) in enumerate(BLOCKS):
                l_ = mm(bank[5 + bi][:, 0:tn], ones, sq[:, t0:t0 + tn], start=first, stop=last_)
            l_.then_inc(rms_mm, 1)

        def transposes(j):
            pe.wait_ge(s_norm, j + 1)
            for i in range(2 * MC):
                last = nc.tensor.transpose(abank(j)[:, i * P:(i + 1) * P], prob[j % 2][:, i * P:(i + 1) * P], ident)
            last.then_inc(t_mm, 1)

        def scores(j):
            t, g = j // 2, j % 2
            if j == 0:
                pe.wait_ge(evac_done, JOB0[1])
            if j >= 3:
                pe.wait_ge(ym_done, j - 2)
            for hp in range(CM):
                last = mm(abank(j)[:, hp * NM:(hp + 1) * NM], qT[g * HD:(g + 1) * HD, hp, t * P:(t + 1) * P],
                          kT[g * HD:(g + 1) * HD, hp, :], start=True, stop=True)
            last.then_inc(s_mm, 1)

        def values(j):
            g = j % 2
            pe.wait_ge(t_copied, j + 1)
            pv = probT[j % 2].rearrange("p (h c t) -> p h c t", h=CM, c=MC)
            for hp in range(CM):
                h = g + 2 * hp
                for c_ in range(MC):
                    last = mm(abank(j)[g * HD:(g + 1) * HD, hp * P:(hp + 1) * P],
                              kv_v[:, c_, D_MEM + h * HD:D_MEM + (h + 1) * HD], pv[:, hp, c_, :],
                              start=c_ == 0, stop=c_ == MC - 1)
            last.then_inc(pv_mm, 1)

        def sample_scores_T():
            pe.wait_ge(ym_done, STEPS - 1)
            pe.wait_ge(q2_ready, 1)
            pe.wait_ge(ld["ckT"], 16)
            sT = abank(STEPS + 1).rearrange("p (g c h b t) -> p g c h b t", g=2, c=MC, h=CM, b=SB)
            for c_ in range(MC):
                for hp in range(CM):
                    for b_ in range(SB):
                        last = mm(sT[:, :, c_, hp, b_, :], ckT[:, b_, hp, c_ * P:(c_ + 1) * P], q2[:, hp, b_, :, :],
                                  start=True, stop=True)
            last.then_inc(stt_mm, 1)

        def sample_scores():
            pe.wait_ge(stt_cp, 1)
            for i in range(2 * MC):
                last = nc.tensor.transpose(abank(STEPS)[:, i * P:(i + 1) * P], st_s[:, i * P:(i + 1) * P], ident)
            last.then_inc(s_mm, 1)

        def sample_values():
            pe.wait_ge(t_copied, STEPS + 1)
            pe.wait_ge(ld["cv"], 16)
            pv = probT[STEPS % 2].rearrange("p (g c h b t) -> p g c h b t", g=2, c=MC, h=CM, b=SB)
            out_ = abank(STEPS)[:, 0:CM * 2 * NS].rearrange("p (h g b t) -> p h g b t", h=CM, g=2, b=SB)
            for hp in range(CM):
                for b_ in range(SB):
                    for c_ in range(MC):
                        last = mm(out_[:, hp, :, b_, :], cv[:, b_, c_, hp * P:(hp + 1) * P], pv[:, :, c_, hp, b_, :],
                                  start=c_ == 0, stop=c_ == MC - 1)
            last.then_inc(pv_mm, 1)

        def attend(r_):
            if r_ < STEPS:
                scores(r_)
            if 2 <= r_ < STEPS + 2:
                values(r_ - 2)
            if 1 <= r_ < STEPS + 1:
                transposes(r_ - 1)
            if r_ == STEPS + 2:
                sample_scores_T()
            if r_ == STEPS + 3:
                sample_scores()
            if r_ == STEPS + 4:
                transposes(STEPS)
            if r_ == STEPS + 5:
                sample_values()

        def after(job):
            if attention_round(job) is not None:
                attend(attention_round(job))
            n = job - JOB0[K_SC]
            if n >= 5 and n % 3 == 2:
                sumsq(n // 3 - 1)

        for k in range(NU):
            project(k, after)
            if K_LRU < k <= K_SC:
                gates(k - 1 - K_LRU)
        for n in range(2 * 3 - 1, len(SUMS)):
            sumsq(n)

        pe.wait_ge(ld["wout"], 16)
        pe.wait_ge(evac_done, JOB0[NU])

        def turn_x1(t):
            pe.wait_ge(x1_done, t + 1)
            if t >= 1:
                pe.wait_ge(xt_cp, t)
            for k in range(KD):
                last = nc.tensor.transpose(ps[:, 2048 + k * P:2048 + (k + 1) * P], x1o[t % 2][:, k * P:(k + 1) * P],
                                           ident)
            last.then_inc(xt_mm, 1)

        def out_project(t, n0, n1):
            for n in range(n0, n1):
                for hf in range(2):
                    last = mm(bank[(t % 2) * 2 + hf], yT[:, SUMS[n], t * P:(t + 1) * P],
                              w_out[:, SUMS[n], hf * 512:(hf + 1) * 512], start=n == 0, stop=n == KD - 1)
            if n1 == KD:
                last.then_inc(op_mm, 1)

        pe.wait_ge(norm_done, 2)
        for t in range(2):
            out_project(t, 0, GROUPS[1][1])
        pe.wait_ge(norm_done, 3)
        out_project(0, GROUPS[1][1], KD)
        out_project(1, GROUPS[1][1], KD)
        turn_x1(0)
        for t in range(2, NL - 1):
            pe.wait_ge(z_done, t - 1)
            out_project(t, 0, KD)
            turn_x1(t - 1)

        def query(route, side):
            R_, tile, h, _ = route
            src = x1Tn if not is_tile0(tile) else x1T0
            if side == 0:
                if is_tile0(tile):
                    pe.wait_ge(ld["x1T0"], 16)
                else:
                    pe.wait_ge(ld["x1T"], tile * 16)
            pe.wait_ge(w_staged, R_ * 2 + (side + 1))
            pe.wait_ge(qt_cp, R_ * 2 + (side + 1))
            for k in range(KD):
                last = mm(bank[2][:, 0:P], wst[side][:, k * P:(k + 1) * P], src[:, k, :], start=k == 0,
                          stop=k == KD - 1)
            last.then_inc(qt_mm, 1)

        def keyscore(route, side):
            R_, tile, h, _ = route
            pe.wait_ge(qt_cp, R_ * 2 + (side + 2))
            pe.wait_ge(sk_used, R_ * 2 + (side + 1))
            mm(bank[3][:, 0:NK], qTs[side], keysT[:, bass.ds(h * (2 * NK) + side * NK, NK)], start=True, stop=True)\
                .then_inc(sk_mm, 1)

        def turn(turn_no, tile, h, routes, tail=False):
            first = turn_no * GRP
            for s in range(GRP):
                pe.wait_ge(diags, first + s + 1)
                pe.wait_ge(gath[s % RING], turn_no * (16 * GRP // RING) + 16 * (s // RING + 1))
                v = ring[s % RING][:, D:2 * D]
                for hf in range(2):
                    last = mm(bank[hf], diag[s % DIAGS], v[:, hf * 512:(hf + 1) * 512], start=False, stop=False)
                last.then_inc(used, 1)
                for r_, side in due(routes, s, QUERY):
                    query(r_, side)
                for r_, side in due(routes, s, KEYS):
                    keyscore(r_, side)

        def open_y(tile):
            pe.wait_ge(y_free, tile + 1)
            for hf in range(2):
                mm(bank[hf], zero[:, :], ln[:, hf * 512:(hf + 1) * 512], start=True, stop=False)

        def close_y(tile):
            for hf in range(2):
                last = mm(bank[hf], zero[:, :], ln[:, hf * 512:(hf + 1) * 512], start=False, stop=True)
            last.then_inc(y_mm, 1)

        pe.wait_ge(ld["keys"], 16)
        pe.nop().then_inc(qt_mm, 2)
        pe.nop().then_inc(sk_mm, 2)
        pe.nop().then_inc(used, RING)
        pe.wait_ge(z_done, NL - 1)

        def lead(h):
            for side in range(2):
                query((h, 0, h, None), side)
                keyscore((h, 0, h, None), side)

        lead(0)
        out_project(NL - 1, 0, KD)
        turn_x1(NL - 2)
        turn_x1(NL - 1)
        for h in range(1, LEAD):
            lead(h)
        pe.wait_ge(pe_zero, 1)
        pe.wait_ge(ld["ln"], 16)
        all_turns(pe, turn, open_y, close_y)

    @block.scalar
    def _(act):
        A_ = nc.scalar.activation
        act.wait_ge(prep_done, 1)
        A_(hb[:, CL:2 * CL], hb[:, 0:CL], ACT.Exp).then_inc(uexp_done, 1)

        def evac(k, after):
            kind, c_, ms = UNITS[k]
            job = JOB0[k]
            for j in range(len(ms)):
                for bi, (t0, tn) in enumerate(BLOCKS):
                    act.wait_ge(proj_done, job + 1)
                    src = bank[job % 3][:, 0:tn]
                    if bi == 0:
                        if kind == "lru" and j == 0 and c_ >= 1:
                            act.wait_ge(conv_done, c_)
                        if kind == "lru" and j == 1 and c_ >= 2:
                            act.wait_ge(y_done, c_ - 1)
                        if kind == "sc" and j == 0 and c_ == 1:
                            act.wait_ge(ym_done, STEPS + 1)
                        if kind == "sc" and j == 1:
                            act.wait_ge(y_done, CL - 1 + c_)
                    if kind == "lru" and j == 0:
                        dst = xlp[:, 3 + t0:3 + min(t0 + tn, SEQ)]
                        if bi == 2:
                            A_(xls[:, :, 3:], src[:, LASTP:].rearrange("p (s t) -> p s t", s=SB), ACT.Copy)
                            src = src[:, 0:LASTP]
                    elif kind == "lru":
                        dst = gg[c_ % 2][:, t0:t0 + tn]
                    elif kind == "sc":
                        dst = (scx, scb, scc)[j][c_][:, t0:t0 + tn]
                    else:
                        dst = qT[:, j, t0:t0 + tn]
                    A_(dst, src, ACT.Gelu if kind == "lru" and j else ACT.Copy).then_inc(evac_done, 1)
                    after(job)
                    job += 1

        def square(n):
            y_k = SUMS[n]
            if y_k < CL + CS:
                act.wait_ge(y_done, y_k + 1)
            else:
                act.wait_ge(ym_done, STEPS + 1)
            if n >= 1:
                act.wait_ge(rms_mm, n)
            A_(sq, yT[:, y_k, 0:NT], ACT.Square).then_inc(sq_done, 1)

        def post_gates(c_):
            if c_ >= 1:
                act.wait_ge(y_done, c_)
            for bi, (t0, tn) in enumerate(BLOCKS):
                for g, (dst, bias) in enumerate(((rb, "b_a"), (ib, "b_x"))):
                    act.wait_ge(gate_mm, (c_ * 3 + bi) * 2 + g + 1)
                    A_(dst[:, t0:t0 + tn], bank[3 + g][:, 0:tn], ACT.Sigmoid, bias=pcol(bias, c_)).then_inc(gate_ev, 1)
            act.wait_ge(gate_ev, (c_ + 1) * 6)
            if c_ == 0:
                act.wait_ge(prep_done, 2)
            A_(rb, rb, ACT.Tanh, scale=hb[:, 7 * CL + c_:7 * CL + c_ + 1]).then_inc(tau_done, 1)
            if c_ >= CL - 2:
                roots(c_)

        def roots(c_):
            act.wait_ge(q_ready, c_ + 1)
            A_(qb, qb, ACT.Sqrt, scale=-1.0).then_inc(root_done, 1)

        def rms(group):
            act.wait_ge(rms_mm, GROUPS[group][1])
            for bi, (t0, tn) in enumerate(BLOCKS):
                last = A_(rmsbuf[group][:, t0:t0 + tn], bank[5 + bi][:, 0:tn], ACT.Sqrt,
                          scale=1.0 / GROUPS[group][2], bias=eps[:, 0:1])
            last.then_inc(rms_root, 1)

        act.wait_ge(kt_done, CM)
        for e in range(CM):
            A_(kT[:, e, :], bank[2 + e][:, 0:NM], ACT.Copy).then_inc(kt_copied, 1)
        act.wait_ge(ld["par"], 16)

        def exps(j):
            o = (j % 2) * 16
            act.wait_ge(s_max, j + 1)
            if j >= 2:
                act.wait_ge(t_mm, j - 1)
            for i in range(2):
                last = A_(prob[j % 2][:, i * NM:(i + 1) * NM], abank(j)[:, i * NM:(i + 1) * NM], ACT.Exp,
                          scale=HD ** -0.5, bias=small[:, o + 4 + i:o + 5 + i], accum_out=small[:, o + 8 + i:o + 9 + i])
            last.then_inc(s_exp, 1)

        def copyT(j):
            act.wait_ge(t_mm, j + 1)
            if j >= 2:
                act.wait_ge(pv_mm, j - 1)
            A_(probT[j % 2], abank(j)[:, 0:2 * NM], ACT.Copy).then_inc(t_copied, 1)

        def attend(r_):
            if 1 <= r_ < STEPS + 1:
                copyT(r_ - 1)
            if r_ < STEPS:
                exps(r_)
            if r_ == STEPS + 2:
                act.wait_ge(stt_mm, 1)
                act.wait_ge(pv_mm, STEPS)
                A_(st_s, abank(STEPS + 1), ACT.Copy).then_inc(stt_cp, 1)
            if r_ == STEPS + 3:
                exps(STEPS)
            if r_ == STEPS + 4:
                copyT(STEPS)

        def after(job):
            if attention_round(job) is not None:
                attend(attention_round(job))
            if job in (JOB0[K_LRU + 2] + 1, JOB0[K_LRU + 3] + 1):
                roots((job - JOB0[K_LRU]) // 6 - 2)
            n = job - JOB0[K_SC]
            if n >= 0 and n % 3 == 2:
                if n // 3 == GROUPS[0][1]:
                    rms(0)
                square(n // 3)

        for k in range(NU):
            evac(k, after)
            if K_LRU < k <= K_SC:
                post_gates(k - 1 - K_LRU)
        rms(1)
        for n in range(2 * 3, len(SUMS)):
            square(n)
        rms(2)

        def dev(t):
            act.wait_ge(var_done, t + 1)
            A_(mv[:, 2:3], mv[:, 1:2], ACT.Sqrt, bias=eps[:, 1:2]).then_inc(sd_done, 1)

        def copy_x1T(t):
            act.wait_ge(xt_mm, t + 1)
            if t >= 2:
                act.wait_ge(st_x1T[t % 2], 16 * (t // 2))
            A_(x1To[t % 2], ps[:, 2048:2048 + D], ACT.Copy).then_inc(xt_cp, 1)

        for t in range(NL - 1):
            dev(t)
            if t >= 1:
                copy_x1T(t - 1)

        def stage(route, side):
            R_, _, h, _ = route
            act.wait_ge(qt_mm, R_ * 2 + (side + 1))
            A_(wst[side], wq[:, bass.ds(h * (2 * KD * DK) + side * (KD * DK), KD * DK)], ACT.Copy)\
                .then_inc(w_staged, 1)

        def copy_q(route, side):
            R_ = route[0]
            act.wait_ge(qt_mm, R_ * 2 + (side + 3))
            act.wait_ge(sk_mm, R_ * 2 + (side + 1))
            A_(qTs[side], bank[2][:, 0:P], ACT.Copy).then_inc(qt_cp, 1)

        act.wait_ge(ld["wq"], 16)
        act.nop().then_inc(qt_cp, 1)
        act.nop().then_inc(gelus, GRP)

        def softmax_exp(k, width=SLOTS):
            act.wait_ge(g_exp_in, k + 1)
            A_(ex[:, 0:width], ex[:, 0:width], ACT.Exp).then_inc(g_exp, 1)

        def next_x1(tile):
            act.wait_ge(ld["x1"], tile * 16 + 16)
            act.wait_ge(x1c_free, tile + 1)
            A_(x1c, x1n, ACT.Copy).then_inc(x1c_ready, 1)

        def dev2(tile):
            act.wait_ge(v2_done, tile + 1)
            A_(mv[:, 2:3], mv[:, 1:2], ACT.Sqrt, bias=eps[:, 1:2]).then_inc(sd2_done, 1)

        def turn(turn_no, tile, h, routes, tail=False):
            first = turn_no * GRP
            sel = fold if isinstance(tile, int) and tile == TILES else ident
            for s in range(GRP):
                act.wait_ge(dots, first + s + 3)
                A_(gel[:, s:s + 1], acts[:, s:s + 1], ACT.Gelu).then_inc(gelus, 1)
                if s == 0:
                    A_(gbuf[:, :], ga_c[:, bass.ds(h * GRP, GRP)], ACT.Copy).then_inc(gates_in, 1)
                    act.wait_ge(gates_in, turn_no + 1)
                act.wait_ge(gelus, first + (s + 1 + GRP))
                A_(wt[:, s:s + 1], gel[:, s:s + 1], ACT.Copy, scale=gbuf[:, s:s + 1]).then_inc(weights, 1)
                act.wait_ge(weights, first + s + 1)
                act.wait_ge(used, first + s + 1 + RING - DIAGS)
                A_(diag[s % DIAGS], sel, ACT.Copy, scale=wt[:, s:s + 1]).then_inc(diags, 1)
                for r_, side in due(routes, s, STAGE):
                    stage(r_, side)
                for r_, side in due(routes, s, COPY_Q):
                    copy_q(r_, side)
                if tail and s == TAIL:
                    dev2(tile - 1)
                for r_, side in due(routes, s, TOP):
                    if side == 1 and is_tile0(r_[1]):
                        softmax_exp(r_[2], TOPK)

        def end(tile):
            if is_tile0(tile):
                softmax_exp(PH)
            elif not (isinstance(tile, int) and tile == TILES):
                softmax_exp(tile + PH)
            if not (isinstance(tile, int) and tile == TILES):
                next_x1(tile + 1)

        def lead(h):
            for side in range(2):
                stage((h, 0, h, None), side)
                copy_q((h, 0, h, None), side)
            softmax_exp(h, TOPK)

        lead(0)
        dev(NL - 1)
        copy_x1T(NL - 2)
        copy_x1T(NL - 1)
        for h in range(1, LEAD):
            lead(h)
        next_x1(0)
        all_turns(act, turn, lambda tile: None, end)
        dev2(TILES)

    @block.vector
    def _(dve):
        V = nc.vector
        chain = Chain(dve, dve_c)
        link, did = chain.link, chain.did
        did(V.memset(eps[:, 0:1], RMS_EPS))
        did(V.memset(eps[:, 1:2], LN_EPS))
        V.memset(zero[:, :], 0.0).then_inc(pe_zero, 1)
        chain.wait()
        dve.wait_ge(ld["par"], 16)
        lam = par[:, PCOL["lam"]:PCOL["lam"] + CL]
        H = [hb[:, i * CL:(i + 1) * CL] for i in range(8)]
        V.scalar_tensor_tensor(H[0], lam, -1.0, lam, ALU.mult, ALU.min).then_inc(prep_done, 1)
        dve.wait_ge(uexp_done, 1)
        link(V.tensor_scalar(H[2], H[1], 2.0, None, ALU.add))
        link(V.reciprocal(H[3], H[2]))
        link(V.tensor_tensor(H[2], H[1], H[3], ALU.mult))
        link(V.tensor_tensor(H[3], H[2], H[2], ALU.mult))
        link(V.tensor_scalar(H[4], H[3], 1.0 / 17, 1.0 / 15, ALU.mult, ALU.add))
        for j in (13, 11, 9, 7, 5, 3, 1):
            link(V.tensor_tensor(H[5], H[4], H[3], ALU.mult))
            link(V.tensor_scalar(H[4], H[5], 1.0 / j, None, ALU.add))
        link(V.tensor_tensor(H[5], H[4], H[2], ALU.mult))
        link(V.tensor_scalar(H[6], lam, -LRU_C / 2, 0.0, ALU.mult, ALU.max))
        V.scalar_tensor_tensor(H[7], H[5], LRU_C, H[6], ALU.mult, ALU.add).then_inc(prep_done, 1)
        for c_ in range(MC):
            dve.wait_ge(kv_done, c_ + 1)
            V.tensor_copy(kv_v[:, c_, :], bank[c_]).then_inc(kv_copied, 1)
        dve.wait_ge(ld["cvst"], 16)
        dve.wait_ge(ld["scst"], 16)
        did(V.memset(xlp[:, 0:3], 0.0))
        chain.wait()

        def save(name, width, c_, src, n_):
            dst = st[:, SCOL[name] + c_ * width:SCOL[name] + (c_ + 1) * width]
            if n_:
                dst = dst.rearrange("p (s t) -> p s t", s=SB)
            return V.tensor_copy(dst, src)

        def taps(out_, buf, halo, w_name, c_, bias, between):
            for j in range(halo + 1):
                wj = pcol(w_name, c_ * (halo + 1) + j)
                for o_, b_, n_ in ((tok(out_)[0], seg(buf, halo)[0], SEQ), (tok(out_)[1], seg(buf, halo)[1], SS)):
                    x_ = b_[:, j:j + n_] if n_ == SEQ else b_[:, :, j:j + n_]
                    if j == 0:
                        if bias is None:
                            did(V.tensor_scalar(o_, x_, wj, None, ALU.mult))
                        else:
                            did(V.tensor_scalar(o_, x_, wj, bias, ALU.mult, ALU.add))
                    else:
                        last = did(V.scalar_tensor_tensor(o_, x_, wj, o_, ALU.mult, ALU.add))
                chain.wait()
                between(j)

        def conv(c_, between):
            did(V.tensor_copy(xls[:, :, 0:3],
                              cvst[:, c_ * SB * 3:(c_ + 1) * SB * 3].rearrange("p (s t) -> p s t", s=SB)))
            chain.wait()
            dve.wait_ge(evac_done, JOB0[K_LRU + c_] + 3)
            did(save("conv_p", 3, c_, xlp[:, SEQ:SEQ + 3], 0))
            did(save("conv_s", SB * 3, c_, xls[:, :, SS:SS + 3], 1))
            if c_ >= 2:
                dve.wait_ge(y_done, c_ - 1)
                dve.wait_ge(gate_mm, (c_ - 1) * 6)
            taps(xc[c_ % 2], xl, 3, "conv_w", c_, pcol("conv_b", c_), between)
            dve.nop().then_inc(conv_done, 1)

        def recur(c_, between):
            dve.wait_ge(tau_done, c_ + 1)
            link(V.tensor_scalar(db, rb, 1.0, None, ALU.add))
            link(V.reciprocal(ab, db))
            link(V.scalar_tensor_tensor(db, rb, 2.0, ab, ALU.mult, ALU.mult))
            did(V.tensor_scalar(ab, db, -1.0, 1.0, ALU.mult, ALU.add))
            V.scalar_tensor_tensor(qb, db, 2.0, db, ALU.subtract, ALU.mult).then_inc(q_ready, 1)
            chain.wait()
            between(0)
            dve.wait_ge(gate_ev, (c_ + 1) * 6)
            link(V.tensor_tensor(ib, ib, xc[c_ % 2], ALU.mult))
            dve.wait_ge(root_done, c_ + 1)
            link(V.tensor_tensor(ib, ib, qb, ALU.mult))
            a0 = tok(ab)[1][:, :, 0]
            b0 = tok(ib)[1][:, :, 0]
            tmp = small[:, 32:32 + SB]
            link(V.tensor_tensor(tmp, a0, par[:, PCOL["h0"] + c_ * SB:PCOL["h0"] + (c_ + 1) * SB], ALU.mult))
            did(V.tensor_tensor(b0, b0, tmp, ALU.add))
            did(V.memset(a0, 0.0))
            chain.wait()
            between(1)
            link(V.tensor_tensor_scan(db, ab, ib, 0.0, ALU.mult, ALU.add))
            did(save("h_p", 1, c_, db[:, SEQ - 1:SEQ], 0))
            did(V.tensor_copy(st[:, SCOL["h_s"] + c_ * SB:SCOL["h_s"] + (c_ + 1) * SB], tok(db)[1][:, :, SS - 1]))
            dve.wait_ge(evac_done, JOB0[K_LRU + c_] + 6)
            link(V.tensor_tensor(yT[:, c_, 0:NT], db, gg[c_ % 2], ALU.mult))
            dve.nop().then_inc(y_done, 1)

        def short_conv(c_):
            if c_ == 0:
                did(V.memset(cxp[:, 0:2], 0.0))
            did(V.tensor_copy(cxs[:, :, 0:2],
                              scst[:, c_ * SB * 2:(c_ + 1) * SB * 2].rearrange("p (s t) -> p s t", s=SB)))
            dve.wait_ge(evac_done, JOB0[K_SC + c_] + 9)
            did(V.tensor_tensor(cxp[:, 2:], tok(scc[c_])[0], tok(scx[c_])[0], ALU.mult))
            did(V.tensor_tensor(cxs[:, :, 2:], tok(scc[c_])[1], tok(scx[c_])[1], ALU.mult))
            chain.wait()
            did(save("sc_p", 2, c_, cxp[:, SEQ:SEQ + 2], 0))
            did(save("sc_s", SB * 2, c_, cxs[:, :, SS:SS + 2], 1))
            taps(yT[:, CL + c_, 0:NT], cx, 2, "sc_w", c_, None, lambda j: None)
            link(V.tensor_tensor(yT[:, CL + c_, 0:NT], yT[:, CL + c_, 0:NT], scb[c_], ALU.mult))
            dve.nop().then_inc(y_done, 1)

        def norm(group):
            dve.wait_ge(rms_root, group + 1)
            link(V.reciprocal(rmsbuf[group], rmsbuf[group]))
            for k in SUMS[GROUPS[group][0]:GROUPS[group][1]]:
                did(V.scalar_tensor_tensor(yT[:, k, 0:NT], yT[:, k, 0:NT], pcol("g", k), rmsbuf[group], ALU.mult,
                                           ALU.mult))
            if group == 2:
                chain.wait()
                link(V.tensor_copy(yT[:, :, NT:NTD], yT[:, :, SEQ:NT]))
            chain.wait()
            dve.nop().then_inc(norm_done, 1)

        def biases(j):
            o = (j % 2) * 16
            dve.wait_ge(s_mm, j + 1)
            link(V.tensor_reduce(small[:, o:o + 2], abank(j).rearrange("p (h m) -> p h m", h=2), AX.X, ALU.max))
            V.tensor_scalar(small[:, o + 4:o + 6], small[:, o:o + 2], -HD ** -0.5, None, ALU.mult).then_inc(s_max, 1)

        def normalize(j):
            o = (j % 2) * 16
            dve.wait_ge(s_exp, j + 1)
            link(V.reciprocal(small[:, o + 12:o + 14], small[:, o + 8:o + 10]))
            for i in range(2):
                pr = prob[j % 2][:, i * NM:(i + 1) * NM]
                did(V.tensor_scalar(pr, pr, small[:, o + 12 + i:o + 13 + i], None, ALU.mult))
            chain.wait()
            dve.nop().then_inc(s_norm, 1)

        def take_y(j):
            lo, t = (j % 2) * HD, j // 2
            dve.wait_ge(pv_mm, j + 1)
            V.tensor_copy(yT[lo:lo + HD, CL + CS:, t * P:(t + 1) * P],
                          abank(j)[lo:lo + HD, 0:CM * P].rearrange("p (c t) -> p c t", c=CM)).then_inc(ym_done, 1)

        def split_queries():
            dve.wait_ge(evac_done, JOB0[1])
            link(V.memset(rmsb[:, 0:CM * SB * 2 * SS], 0.0))
            for g in range(2):
                lo = g * HD
                for hp in range(CM):
                    did(V.tensor_copy(q2[lo:lo + HD, hp, :, g, :],
                                      qT[lo:lo + HD, hp, SEQ:NT].rearrange("p (b t) -> p b t", b=SB)))
            chain.wait()
            dve.nop().then_inc(q2_ready, 1)

        def take_sample_y():
            dve.wait_ge(pv_mm, STEPS + 1)
            out_ = abank(STEPS)[:, 0:CM * 2 * NS].rearrange("p (h g n) -> p h g n", h=CM, g=2)
            for g in range(2):
                did(V.tensor_copy(yT[g * HD:(g + 1) * HD, CL + CS:, SEQ:NT], out_[g * HD:(g + 1) * HD, :, g, :]))
            chain.wait()
            dve.nop().then_inc(ym_done, 1)

        def attend(r_):
            if 1 <= r_ < STEPS + 1:
                normalize(r_ - 1)
            if r_ < STEPS:
                biases(r_)
            if 2 <= r_ < STEPS + 2:
                take_y(r_ - 2)
            if r_ == 2:
                split_queries()
            if r_ == STEPS + 3:
                biases(STEPS)
            if r_ == STEPS + 4:
                normalize(STEPS)
            if r_ == STEPS + 5:
                take_sample_y()

        for c_ in range(CL):
            attend(6 * c_)
            if c_ >= 2:
                recur(c_ - 2, lambda j: attend(6 * c_ + 1 + j))
            else:
                attend(6 * c_ + 1)
                attend(6 * c_ + 2)
            conv(c_, lambda j: attend(6 * c_ + 3 + j) if j < 3 else None)
        for c_ in (CL - 2, CL - 1):
            recur(c_, lambda j: None)
        short_conv(0)
        norm(0)
        short_conv(1)
        norm(1)
        norm(2)
        dve.nop().then_inc(mixer_done, 1)

        def layernorm(x_, psum, z, dst, gi, var_sem, sd_sem, tile, zsem):
            ins = V.scalar_tensor_tensor(z, x_, ALPHA, psum, ALU.mult, ALU.add)
            link(ins)
            dve.nop().then_inc(zsem, 1)
            for hf in range(2):
                did(V.bn_stats(bst[:, hf * 6:(hf + 1) * 6], z[:, hf * 512:(hf + 1) * 512]))
            chain.wait()
            link(V.bn_aggr(mv[:, 0:2], bst[:, :]))
            dve.nop().then_inc(var_sem, 1)
            dve.wait_ge(sd_sem, tile + 1)
            link(V.reciprocal(mv[:, 3:4], mv[:, 2:3]))
            link(V.tensor_scalar(z, z, mv[:, 0:1], mv[:, 3:4], ALU.subtract, ALU.mult))
            link(V.tensor_tensor(z, z, ln_v[:, gi, :], ALU.mult))
            link(V.tensor_tensor(dst, z, ln_v[:, gi + 1, :], ALU.add))

        def layernorm1(t):
            dve.wait_ge(op_mm, t + 1)
            dve.wait_ge(ld_xt[t % 2], 16 * (t // 2 + 1))
            if t >= 2:
                dve.wait_ge(st_x1[t % 2], 16 * (t // 2))
                dve.wait_ge(xt_mm, t - 1)
            layernorm(xt[t % 2], ps[:, (t % 2) * D:(t % 2 + 1) * D], x1o[t % 2], x1o[t % 2], 0, var_done, sd_done, t,
                      z_done)
            dve.nop().then_inc(x1_done, 1)

        dve.wait_ge(ld["ln"], 16)
        for t in range(NL - 1):
            layernorm1(t)

        for s_ in (sk_used, x1c_free):
            dve.nop().then_inc(s_, 1)
        dve.nop().then_inc(dots, len(junk))

        def top16(scr, src, vals, inds, src_read=None):
            link(V.max(vals[:, 0:8], src))
            did(V.max_index(inds[:, 0:8], vals[:, 0:8], src))
            link(V.match_replace(scr, vals[:, 0:8], src, LOW))
            if src_read is not None:
                dve.nop().then_inc(src_read, 1)
            link(V.max(vals[:, 8:16], scr))
            link(V.max_index(inds[:, 8:16], vals[:, 8:16], scr))

        def side_top(route, side):
            dve.wait_ge(sk_mm, route[0] * 2 + (side + 3))
            dve.sem_inc(dve_turned, 1)
            top16(sk2, bank[3][:, 0:NK], val[:, side * TOPK:(side + 1) * TOPK], idx[:, side * TOPK:(side + 1) * TOPK],
                  sk_used)

        def b3(ap, inner):
            return (ap.unsqueeze(2) if inner else ap.unsqueeze(1)).broadcast_to([P, TOPK, TOPK])

        def head_top(route):
            v3 = cand[0].rearrange("p (i j) -> p i j", i=TOPK)
            oh = onehot.rearrange("p (i j) -> p i j", i=TOPK)
            did(V.tensor_copy(idxf[:, :], idx[:, :]))
            link(V.tensor_tensor(v3, b3(val[:, 0:TOPK], True), b3(val[:, TOPK:], False), ALU.add))
            top16(cand[1], cand[0], top, ci)
            did(V.tensor_scalar(ch[:, 0:TOPK], ci[:, :], 4, None, ALU.logical_shift_right))
            did(V.tensor_scalar(ch[:, TOPK:], ci[:, :], TOPK - 1, None, ALU.bitwise_and))
            chain.wait()
            for sd in range(2):
                link(V.tensor_tensor(oh, b3(ch[:, sd * TOPK:(sd + 1) * TOPK], True), b3(iota16, False), ALU.is_equal))
                link(V.tensor_tensor(oh, oh, b3(idxf[:, sd * TOPK:(sd + 1) * TOPK], False), ALU.mult))
                link(V.tensor_reduce(ef[:, sd * TOPK:(sd + 1) * TOPK], oh, AX.X, ALU.add))
            link(V.scalar_tensor_tensor(eu[:, :], ef[:, 0:TOPK], float(NK), ef[:, TOPK:], ALU.mult, ALU.add))
            if is_tile0(route[1]):
                tile0_gates(route[2])
                return
            for lo, hh in ((0, route[2]), (P // 2, (route[2] + PH // 2) % PH)):
                did(V.tensor_copy(idx_w[lo:lo + P // 2, bass.ds(hh * TOPK + SLOTS, TOPK)], eu[lo:lo + P // 2, :]))
                did(V.tensor_copy(sc_n[lo:lo + P // 2, bass.ds(hh * TOPK, TOPK)], top[lo:lo + P // 2, :]))
            chain.wait()

        def tile0_gates(h):
            did(V.tensor_copy(idx_w[:, bass.ds(h * TOPK, TOPK)], eu[:, :]))
            link(V.tensor_scalar(ex[:, 0:TOPK], top[:, :], top[:, 0:1], None, ALU.subtract))
            dve.nop().then_inc(g_exp_in, 1)
            dve.wait_ge(g_exp, h + 1)
            link(V.tensor_reduce(den[:, 0:1], ex[:, 0:TOPK], AX.X, ALU.add))
            link(V.reciprocal(den[:, 1:2], den[:, 0:1]))
            link(V.tensor_scalar(ga_c[:, bass.ds(h * TOPK, TOPK)], ex[:, 0:TOPK], den[:, 1:2], None, ALU.mult))

        def promote(tile):
            s3 = sc_n[:, :].rearrange("p (h k) -> p h k", h=PH)
            e3 = ex[:, :].rearrange("p (h k) -> p h k", h=PH)
            did(V.tensor_copy(idx_w[:, 0:SLOTS], idx_w[:, SLOTS:]))
            link(V.tensor_tensor(e3, s3, s3[:, :, 0:1].broadcast_to([P, PH, TOPK]), ALU.subtract))
            dve.nop().then_inc(g_exp_in, 1)
            dve.wait_ge(g_exp, tile + PH)
            link(V.tensor_reduce(den[:, 0:PH], e3, AX.X, ALU.add))
            link(V.reciprocal(den[:, PH:], den[:, 0:PH]))
            link(V.tensor_tensor(ga_c[:, :].rearrange("p (h k) -> p h k", h=PH), e3,
                                 den[:, PH:].unsqueeze(2).broadcast_to([P, PH, TOPK]), ALU.mult))

        def turn(turn_no, tile, h, routes, tail=False):
            first = turn_no * GRP
            chain.restart()
            dve.wait_ge(x1c_ready, tile + 1)
            for s in range(GRP):
                if s % RING == 0:
                    dve.wait_ge(gelus, first + (s + RING))
                dve.wait_ge(dots, first + s + 1)
                dve.wait_ge(gath[s % RING], turn_no * (16 * GRP // RING) + 16 * (s // RING + 1))
                V.tensor_tensor_reduce(out=junk[s % 2], in0=ring[s % RING][:, 0:D], in1=x1c, scale=1.0, scalar=0.0,
                                       op0=ALU.mult, op1=ALU.add, accum_out=acts[:, s:s + 1]).then_inc(dots, 1)
                if s % RING == RING - 1:
                    V.tensor_copy(ibuf[s // RING][:, :], idx_w[:, bass.ds(h * GRP + (GRP + s + 1 - RING), RING)])\
                        .then_inc(idx_ready, 1)
                sides = due(routes, s, TOP)
                if s == GRP - 1:
                    sides = [x for s_ in range(s, s + GRP) for x in due(routes, s_, TOP)]
                for r_, side in sides:
                    side_top(r_, side)
                    if side == 1:
                        head_top(r_)
                if tail and s == TAIL:
                    finish(tile - 1)

        def residual(tile):
            dve.wait_ge(y_mm, tile + 1)
            dve.wait_ge(yo_free, tile + 1)
            link(V.scalar_tensor_tensor(yout, x1c, ALPHA, ps[:, 0:D], ALU.mult, ALU.add))
            dve.nop().then_inc(y_free, 1)
            dve.nop().then_inc(x1c_free, 1)

        def finish(tile):
            for hf in range(2):
                did(V.bn_stats(bst[:, hf * 6:(hf + 1) * 6], yout[:, hf * 512:(hf + 1) * 512]))
            chain.wait()
            link(V.bn_aggr(mv[:, 0:2], bst[:, :]))
            dve.nop().then_inc(v2_done, 1)
            dve.wait_ge(sd2_done, tile + 1)
            link(V.reciprocal(mv[:, 3:4], mv[:, 2:3]))
            link(V.tensor_scalar(yout, yout, mv[:, 0:1], mv[:, 3:4], ALU.subtract, ALU.mult))
            link(V.tensor_tensor(yout, yout, ln_v[:, 2, :], ALU.mult))
            link(V.tensor_tensor(yout, yout, ln_v[:, 3, :], ALU.add))
            dve.nop().then_inc(yo_ready, 1)

        def end(tile):
            chain.restart()
            if not (isinstance(tile, int) and tile == TILES):
                promote(tile + 1)
            residual(tile)

        def lead(h):
            chain.wait()
            chain.restart()
            for side in range(2):
                side_top((h, 0, h, None), side)
            head_top((h, 0, h, None))

        lead(0)
        for i in range(2):
            V.tensor_copy(ibuf[i][:, :], idx_w[:, i * RING:(i + 1) * RING]).then_inc(idx_ready, 1)
        layernorm1(NL - 1)
        dve.nop().then_inc(y_free, 1)
        for h in range(1, LEAD):
            lead(h)
        dve.wait_ge(ld["x1"], 16)
        all_turns(dve, turn, lambda tile: None, end)
        finish(TILES)

    for x in reversed(ctx):
        x.__exit__(None, None, None)


INPUTS = ["consts", "par", "cvst", "scst", "wrg", "memT", "wkv", "w_in", "xT", "w_out", "ln", "ckT", "cv", "x_tok",
          "wq", "keys", "uv"]


def kernel(**inp):
    import concourse.bacc as bacc
    from concourse.bass_utils import run_bass_kernel_spmd

    i = {k: np.asarray(v) for k, v in inp.items()}

    def cols(v, n):
        v = v.reshape(-1, n, P)
        return np.ascontiguousarray(v.transpose(2, 1, 0).reshape(P, -1))

    xs = i["x_sample"].reshape(NS, D)
    x_tok = np.concatenate([i["x_prompt"][0], xs, xs])
    xT = np.concatenate([i["x_prompt"][0], xs]).T

    def by_k(m):
        return np.ascontiguousarray(m.reshape(-1, P, m.shape[1]).transpose(1, 0, 2))

    wrg = np.zeros((P, CL, 2, P), np.float32)
    for g, name in enumerate(("w_rg_a", "w_rg_x")):
        for h in range(2 * CL):
            lo = HD * (h % 2)
            wrg[lo:lo + HD, h // 2, g, lo:lo + HD] = i[name][0, h]
    par = np.concatenate([
        cols(i["lru_conv_w"][0], CL), cols(i["lru_conv_b"][0], CL), cols(i["b_rg_a"][0], CL),
        cols(i["b_rg_x"][0], CL), cols(i["lru_lambda"][0], CL), cols(i["sc_conv_w"][0], CS),
        cols(i["g_lru"][0], CL), cols(i["g_sc"][0], CS), cols(i["g_mem"][0], CM),
        cols(i["state_lru_h"][0], CL)], axis=1)
    half = np.arange(P) % NS
    consts = np.concatenate([np.eye(P), half[:, None] == half[None, :], np.ones((P, P)),
                             np.tile(np.arange(TOPK), (P, 1))], axis=1).astype(np.float32)
    w_in = i["w_in"][0].reshape(KD, P, -1, P).transpose(2, 1, 0, 3)
    ck = i["cache_mem_k"][0].reshape(SB, NM, CM, P).transpose(3, 0, 2, 1)
    cv = i["cache_mem_v"][0].reshape(SB, MC, P, D_MEM).transpose(2, 0, 1, 3)
    wq = i["peer_wq"][0].reshape(KD, P, SIDES, DK).transpose(1, 2, 0, 3)
    keys = i["peer_keys"][0].reshape(SIDES, NK, DK).transpose(2, 0, 1)
    arrays = {
        "consts": consts, "par": par, "cvst": cols(i["state_lru_conv"][0], CL),
        "scst": cols(i["state_sc_conv"][0], CS), "wrg": wrg.reshape(P, -1),
        "memT": by_k(i["mem_prompt"][0].T), "wkv": by_k(i["w_mem_kv"][0]), "w_in": w_in, "xT": by_k(xT),
        "w_out": by_k(i["w_out"][0]),
        "ln": np.stack([i["ln1_g"][0], i["ln1_b"][0], i["ln2_g"][0], i["ln2_b"][0]]),
        "ckT": ck, "cv": cv, "x_tok": x_tok.reshape(TILES + 1, P, D),
        "wq": wq.reshape(P, -1), "keys": keys.reshape(P, -1),
        "uv": np.concatenate([i["peer_u"][0], i["peer_v"][0]], axis=1),
    }
    nc = bacc.Bacc("TRN2", target_bir_lowering=False, num_devices=1)
    A, feeds = {}, {}
    for name in INPUTS:
        arr = np.ascontiguousarray(arrays[name], dtype=np.float32)
        feeds["in_" + name] = arr
        A[name] = nc.dram_tensor("in_" + name, arr.shape, F32, kind="ExternalInput").ap()
    O = {}
    for name, shape in (("kv", (NM, 2 * D_MEM)), ("states", (P, NST)), ("y", ((TILES + 1) * P, D))):
        O[name] = nc.dram_tensor("out_" + name, shape, F32, kind="ExternalOutput").ap()
    for name in ("x1", "x1T"):
        O[name] = nc.dram_tensor("scratch_" + name, ((TILES + 1) * P, D), F32).ap()
    build(nc, A, O)
    r = run_bass_kernel_spmd(nc, [feeds], core_ids=[0]).results[0]
    y, kv, st = r["out_y"], r["out_kv"], r["out_states"]

    def state(name, n, *rest):
        w = n * int(np.prod(rest, dtype=int))
        v = st[:, SCOL[name]:SCOL[name] + w].reshape(P, n, *rest)
        axes = list(range(2, 2 + len(rest))) + [1, 0]
        return np.ascontiguousarray(v.transpose(axes)).reshape(*rest, n * P)

    return (
        y[:SEQ].reshape(1, SEQ, D), y[SEQ:SEQ + NS].reshape(SB, SS, D),
        kv[:, :D_MEM].reshape(1, 1, NM, MH, HD), kv[:, D_MEM:].reshape(1, 1, NM, MH, HD),
        state("conv_p", CL, 3)[None, None], state("h_p", CL, 1)[None], state("sc_p", CS, 2)[None, None],
        state("conv_s", CL, SB, 3)[None], state("h_s", CL, SB)[None], state("sc_s", CS, SB, 2)[None])
```
